# Optimizing a Trainium2 kernel written in Bass

```python
import jax
import jax.numpy as jnp
from jax import lax
import numpy as np
import math
import jax, jax.numpy as jnp

D_MODEL = 1024
BATCH = 1
SEQ = 256
DEPTH = 1

CTX_LEN = 256
GRID_W = 64
FOURIER_W = 512
FOURIER_GROUPS = 8
RWKV_W = D_MODEL - FOURIER_W
HEAD = 64
N_HEADS = RWKV_W // HEAD
N_DIR = 2
DECAY_RANK = 64
ICLR_RANK = 64
GATE_RANK = 128
D_FF = 2816
RWKV_PROJ_W = 3 * RWKV_W + N_DIR * DECAY_RANK + N_DIR * ICLR_RANK + GATE_RANK
PROJ_W = FOURIER_W + RWKV_PROJ_W
NORM_EPS = 1e-6
GN_EPS = 64e-5
KK_EPS = 1e-12


def rms_norm(x, g):
    xf = x.astype(jnp.float32)
    y = xf * lax.rsqrt(jnp.mean(xf * xf, axis=-1, keepdims=True) + NORM_EPS)
    return (y * g.astype(jnp.float32)).astype(x.dtype)

def modulate(h, shift, scale):
    return h * (1 + scale) + shift

def conv1d_centred(u, w):
    up = jnp.pad(u, ((0, 0), (1, 1), (0, 0)))
    return up[:, :-2] * w[0] + up[:, 1:-1] * w[1] + up[:, 2:] * w[2]

def conv2d_grid(u, w, rows):
    b, t, ch = u.shape
    g = u.reshape(b, rows, GRID_W, ch)
    y = lax.conv_general_dilated(g, w[:, :, None, :].astype(u.dtype), (1, 1), "SAME",
                                 dimension_numbers=("NHWC", "HWIO", "NHWC"),
                                 feature_group_count=ch)
    return y.reshape(b, t, ch)

def fourier_mix(u, g):
    b, t, _ = u.shape
    uf = u.astype(jnp.float32).reshape(b, t, FOURIER_GROUPS, FOURIER_W // FOURIER_GROUPS)
    y = jnp.fft.fft2(uf, axes=(1, 3), norm="ortho").real
    return rms_norm(y.reshape(b, t, FOURIER_W), g).astype(u.dtype)

def rwkv_inputs(u, conv_w, w0, w2, a0, a2, k_k, k_a):
    b, t, _ = u.shape
    rkv = conv1d_centred(u[..., :3 * RWKV_W], conv_w)
    r, k, v = jnp.split(rkv, 3, axis=-1)
    o = 3 * RWKV_W
    wd = u[..., o:o + N_DIR * DECAY_RANK].reshape(b, t, N_DIR, DECAY_RANK)
    o += N_DIR * DECAY_RANK
    ad = u[..., o:o + N_DIR * ICLR_RANK].reshape(b, t, N_DIR, ICLR_RANK)
    o += N_DIR * ICLR_RANK
    gd = u[..., o:]
    w_lora = (w0 + jnp.einsum("btdr,drc->btdc", jnp.tanh(wd), w2)).astype(jnp.float32)
    decay = jnp.exp(-jnp.exp(-jax.nn.softplus(-w_lora) - 0.5))
    a = jax.nn.sigmoid((a0 + jnp.einsum("btdr,drc->btdc", ad, a2)).astype(jnp.float32))
    kk = (k * k_k).astype(jnp.float32).reshape(b, t, N_HEADS, HEAD)
    kk = kk * lax.rsqrt(jnp.sum(kk * kk, axis=-1, keepdims=True) + KK_EPS)
    kk = kk.reshape(b, t, RWKV_W)
    kd = k.astype(jnp.float32)[:, :, None] * (1 + (a - 1) * k_a)
    return r, kd, v, kk, a, decay, gd

def _heads_time_major(x2):
    d, b, t, _ = x2.shape
    return x2.astype(jnp.float32).reshape(d, b, t, N_HEADS, HEAD).transpose(2, 0, 1, 3, 4)

def shared_dirs(x):
    return _heads_time_major(jnp.stack([x, jnp.flip(x, axis=1)], axis=0))

def per_dir(x):
    return _heads_time_major(jnp.stack([x[:, :, 0], jnp.flip(x[:, :, 1], axis=1)], axis=0))

def merge_dirs(y):
    y = y.transpose(1, 2, 0, 3, 4)
    return y[0] + jnp.flip(y[1], axis=1)

def rwkv_scan(prep, state0, readout):
    r, kd, v, kk, a, decay, _ = prep
    xs = (shared_dirs(r), per_dir(kd), shared_dirs(v), shared_dirs(kk), per_dir(a), per_dir(decay))

    def step(s, inp):
        r_t, k_t, v_t, kk_t, a_t, w_t = inp
        sa = jnp.einsum("dbhij,dbhj->dbhi", s, kk_t)
        s = (s * w_t[..., None, :] - sa[..., :, None] * (kk_t * a_t)[..., None, :]
             + v_t[..., :, None] * k_t[..., None, :])
        y = jnp.einsum("dbhij,dbhj->dbhi", s, r_t) if readout else None
        return s, y

    return lax.scan(step, state0, xs)

def rwkv_output(y, prep, g2, r_k, gn_g, gn_b):
    r, kd, v, _, _, _, gd = prep
    b, t = r.shape[:2]
    mu = jnp.mean(y, axis=-1, keepdims=True)
    var = jnp.mean(jnp.square(y - mu), axis=-1, keepdims=True)
    yn = ((y - mu) * lax.rsqrt(var + GN_EPS)).reshape(b, t, RWKV_W)
    yn = yn * gn_g.astype(jnp.float32) + gn_b.astype(jnp.float32)
    rh = r.astype(jnp.float32).reshape(b, t, N_HEADS, HEAD)
    vh = v.astype(jnp.float32).reshape(b, t, N_HEADS, HEAD)
    kdh = kd.reshape(b, t, N_DIR, N_HEADS, HEAD)
    bonus = jnp.einsum("bthn,btdhn,hn->bth", rh, kdh, r_k.astype(jnp.float32))[..., None] * vh
    gate = jax.nn.sigmoid(gd.astype(jnp.float32)) @ g2.astype(jnp.float32)
    return (yn + bonus.reshape(b, t, RWKV_W)) * gate

def token_mixer(h, hc, w_in, conv_w, w0, w2, a0, a2, g2, k_k, k_a, r_k, gn_g, gn_b,
                f_g, w_out, ctx_out):
    u = h @ w_in
    uc = hc @ (w_in if ctx_out else w_in[:, FOURIER_W:])
    uc_r = uc[..., FOURIER_W:] if ctx_out else uc
    prep_l = rwkv_inputs(u[..., FOURIER_W:], conv_w, w0, w2, a0, a2, k_k, k_a)
    prep_c = rwkv_inputs(uc_r, conv_w, w0, w2, a0, a2, k_k, k_a)
    state0 = jnp.zeros((N_DIR, hc.shape[0], N_HEADS, HEAD, HEAD), jnp.float32)
    state_c, y_c = rwkv_scan(prep_c, state0, ctx_out)
    _, y_l = rwkv_scan(prep_l, state_c, True)
    rw_l = rwkv_output(merge_dirs(y_l), prep_l, g2, r_k, gn_g, gn_b).astype(h.dtype)
    out = jnp.concatenate([fourier_mix(u[..., :FOURIER_W], f_g).astype(h.dtype), rw_l], axis=-1) @ w_out
    out_c = None
    if ctx_out:
        rw_c = rwkv_output(merge_dirs(y_c), prep_c, g2, r_k, gn_g, gn_b).astype(hc.dtype)
        out_c = jnp.concatenate([fourier_mix(uc[..., :FOURIER_W], f_g).astype(hc.dtype), rw_c], axis=-1) @ w_out
    return out, out_c

def conv_ffn(h, w_up, conv_w, conv_b, w_down, rows):
    u = h @ w_up
    if rows is None:
        u = conv1d_centred(u, conv_w[1]) + conv_b
    else:
        u = conv2d_grid(u, conv_w, rows) + conv_b
    gate, val = jnp.split(u, 2, axis=-1)
    return (jax.nn.silu(gate) * val) @ w_down

def first_inputs(seed: int = 0) -> dict:
    key = jax.random.key(seed)
    ks = jax.random.split(key, 27)
    L, D, C, F2 = DEPTH, D_MODEL, RWKV_W, 2 * D_FF

    def nrm(i, shape, s=1.0):
        return s * jax.random.normal(ks[i], shape, jnp.float32)

    def near_one(i, shape):
        return 1.0 + nrm(i, shape, 0.05)

    centre3 = jnp.zeros((3,), jnp.float32).at[1].set(1.0)
    centre33 = jnp.zeros((3, 3), jnp.float32).at[1, 1].set(1.0)
    return {
        "x": nrm(0, (BATCH, SEQ, D)),
        "c": nrm(1, (BATCH, D)),
        "ctx": nrm(2, (BATCH, CTX_LEN, D)),
        "c_ctx": nrm(3, (D,)),
        "ada_w": nrm(4, (L, D, 6 * D), 0.5 * D ** -0.5),
        "ada_b": nrm(5, (L, 6 * D), 0.02),
        "norm1_g": near_one(6, (L, D)),
        "norm2_g": near_one(7, (L, D)),
        "w_in": nrm(8, (L, D, PROJ_W), D ** -0.5),
        "rwkv_conv_w": centre3[None, :, None] + nrm(9, (L, 3, 3 * C), 0.1),
        "decay_w0": -1.0 + nrm(10, (L, N_DIR, C), 1.5),
        "decay_w2": nrm(11, (L, N_DIR, DECAY_RANK, C), 0.1 * DECAY_RANK ** -0.5),
        "iclr_a0": nrm(12, (L, N_DIR, C), 0.5),
        "iclr_a2": nrm(13, (L, N_DIR, ICLR_RANK, C), 0.1 * ICLR_RANK ** -0.5),
        "gate_g2": nrm(14, (L, GATE_RANK, C), GATE_RANK ** -0.5),
        "k_k": 0.85 + nrm(15, (L, C), 0.05),
        "k_a": near_one(16, (L, C)),
        "r_k": nrm(17, (L, N_HEADS, HEAD), 0.1),
        "gn_g": near_one(18, (L, C)),
        "gn_b": nrm(19, (L, C), 0.02),
        "fourier_g": near_one(20, (L, FOURIER_W)),
        "w_out": nrm(21, (L, D, D), D ** -0.5),
        "ffn_w_up": nrm(22, (L, D, F2), D ** -0.5),
        "ffn_conv_w": centre33[None, :, :, None] + nrm(23, (L, 3, 3, F2), 0.1),
        "ffn_conv_b": nrm(24, (L, F2), 0.02),
        "ffn_w_down": nrm(25, (L, D_FF, D), D_FF ** -0.5),
        "final_g": near_one(26, (D,)),
    }

def first_block(x, c, ctx, c_ctx, ada_w, ada_b, norm1_g, norm2_g, w_in, rwkv_conv_w,
              decay_w0, decay_w2, iclr_a0, iclr_a2, gate_g2, k_k, k_a, r_k, gn_g, gn_b,
              fourier_g, w_out, ffn_w_up, ffn_conv_w, ffn_conv_b, ffn_w_down, final_g):
    rows = x.shape[1] // GRID_W
    for l in range(DEPTH):
        last = l == DEPTH - 1
        mod_x = jax.nn.silu(c) @ ada_w[l] + ada_b[l]
        mod_c = jax.nn.silu(c_ctx) @ ada_w[l] + ada_b[l]
        sh1, sc1, g1, sh2, sc2, g2 = [m[:, None, :] for m in jnp.split(mod_x, 6, axis=-1)]
        sh1c, sc1c, g1c, sh2c, sc2c, g2c = jnp.split(mod_c, 6, axis=-1)

        h = modulate(rms_norm(x, norm1_g[l]), sh1, sc1)
        hc = modulate(rms_norm(ctx, norm1_g[l]), sh1c, sc1c)
        y, yc = token_mixer(h, hc, w_in[l], rwkv_conv_w[l], decay_w0[l], decay_w2[l],
                            iclr_a0[l], iclr_a2[l], gate_g2[l], k_k[l], k_a[l], r_k[l],
                            gn_g[l], gn_b[l], fourier_g[l], w_out[l], not last)
        x = x + g1 * y
        h = modulate(rms_norm(x, norm2_g[l]), sh2, sc2)
        x = x + g2 * conv_ffn(h, ffn_w_up[l], ffn_conv_w[l], ffn_conv_b[l], ffn_w_down[l], rows)
        if not last:
            ctx = ctx + g1c * yc
            hc = modulate(rms_norm(ctx, norm2_g[l]), sh2c, sc2c)
            ctx = ctx + g2c * conv_ffn(hc, ffn_w_up[l], ffn_conv_w[l], ffn_conv_b[l],
                                       ffn_w_down[l], None)
    return rms_norm(x, final_g)


N_META = 16
Q_BLOCK = 128
EPS = 1e-6

A_HEADS = 8
A_HEAD_DIM = 64
A_QK_WIDTH = A_HEADS * 2 * A_HEAD_DIM
A_V_WIDTH = A_HEADS * 2 * A_HEAD_DIM

B_HEADS = 8
B_KV_HEADS = 2
B_GROUP = B_HEADS // B_KV_HEADS
B_HEAD_DIM = 128
B_Q_WIDTH = B_HEADS * B_HEAD_DIM
B_KV_WIDTH = B_KV_HEADS * B_HEAD_DIM
ROPE_THETA = 10000.0

SPLITS = (A_QK_WIDTH, A_QK_WIDTH, A_V_WIDTH, B_Q_WIDTH, B_KV_WIDTH, B_KV_WIDTH, D_MODEL, D_MODEL)
IN_WIDTH = sum(SPLITS)

N_EXPERTS = 16
EXPERT_FF = 512
CAPACITY_FACTOR = 2


def rms_norm_2(x, g):
    xf = x.astype(jnp.float32)
    y = xf * lax.rsqrt(jnp.mean(xf * xf, axis=-1, keepdims=True) + EPS)
    return (y * g.astype(jnp.float32)).astype(x.dtype)

def sweep_queries(block_fn, *qs):
    out_meta = block_fn(*[a[:, :N_META] for a in qs])

    def to_blocks(a):
        r = a[:, N_META:]
        n = r.shape[1] // Q_BLOCK
        r = r.reshape((r.shape[0], n, Q_BLOCK) + r.shape[2:])
        return jnp.moveaxis(r, 1, 0)

    out_real = lax.map(lambda args: block_fn(*args), tuple(to_blocks(a) for a in qs))
    out_real = jnp.moveaxis(out_real, 0, 1)
    out_real = out_real.reshape((out_real.shape[0], -1) + out_real.shape[3:])
    return jnp.concatenate([out_meta, out_real], axis=1)

def alibi_slopes(n_heads):
    return jnp.exp2(-8.0 * jnp.arange(1, n_heads + 1, dtype=jnp.float32) / n_heads)

def diff_attention(q, k, v, pos, slopes, lam):
    scale = A_HEAD_DIM ** -0.5
    k_meta = pos < N_META

    def block(qb, pb):
        qp = pb[0]
        s = jnp.einsum('bqhmd,bkhmd->bhmqk', qb, k).astype(jnp.float32) * scale
        dist = jnp.abs(qp[:, None] - pos[None, :]).astype(jnp.float32)
        dist = jnp.where((qp[:, None] < N_META) | k_meta[None, :], 0.0, dist)
        s = s - slopes[None, :, None, None, None] * dist
        p = jax.nn.softmax(s, axis=-1)
        w = p[:, :, 0] - lam * p[:, :, 1]
        return jnp.einsum('bhqk,bkhe->bqhe', w.astype(v.dtype), v)

    return sweep_queries(block, q, pos[None])

def gqa_attention(q, k, v):
    scale = B_HEAD_DIM ** -0.5

    def block(qb):
        s = jnp.einsum('bqngd,bknd->bngqk', qb, k).astype(jnp.float32) * scale
        p = jax.nn.softmax(s, axis=-1)
        return jnp.einsum('bngqk,bknd->bqngd', p.astype(v.dtype), v)

    return sweep_queries(block, q)

def axial_angles(total_len):
    n_tok = total_len - N_META
    rows = n_tok // GRID_W
    row_id = jnp.repeat(jnp.arange(rows, dtype=jnp.int32), GRID_W)
    col_id = jnp.tile(jnp.arange(GRID_W, dtype=jnp.int32), rows)
    zeros = jnp.zeros((N_META,), jnp.int32)
    row_id = jnp.concatenate([zeros, row_id])
    col_id = jnp.concatenate([zeros, col_id])
    half = B_HEAD_DIM // 2
    inv_freq = ROPE_THETA ** (-jnp.arange(0, half, 2, dtype=jnp.float32) / half)
    return (row_id.astype(jnp.float32)[:, None] * inv_freq[None, :],
            col_id.astype(jnp.float32)[:, None] * inv_freq[None, :])

def rotate(x, ang):
    m = ang.shape[-1]
    cos = jnp.cos(ang)[None, :, None, :].astype(x.dtype)
    sin = jnp.sin(ang)[None, :, None, :].astype(x.dtype)
    x1, x2 = x[..., :m], x[..., m:]
    return jnp.concatenate([x1 * cos - x2 * sin, x2 * cos + x1 * sin], axis=-1)

def axial_rope(x, ang_row, ang_col):
    half = x.shape[-1] // 2
    return jnp.concatenate([rotate(x[..., :half], ang_row), rotate(x[..., half:], ang_col)], axis=-1)

def expert_choice_ffn(u, w_router, w_gate, w_up, w_down):
    b, L, d = u.shape
    cap = CAPACITY_FACTOR * L // N_EXPERTS
    logits = jnp.einsum('bld,de->ble', u, w_router).astype(jnp.float32)
    aff = jax.nn.softmax(logits, axis=-1)
    top_aff, top_idx = lax.top_k(jnp.swapaxes(aff, 1, 2), cap)
    xs = jax.vmap(lambda ub, ib: ub[ib])(u, top_idx)
    hid = jax.nn.silu(jnp.einsum('becd,edf->becf', xs, w_gate)) * jnp.einsum('becd,edf->becf', xs, w_up)
    y = jnp.einsum('becf,efd->becd', hid, w_down) * top_aff[..., None].astype(u.dtype)
    return jax.vmap(lambda yb, ib: jnp.zeros((L, d), yb.dtype).at[ib.reshape(-1)].add(yb.reshape(-1, d)))(y, top_idx)

def second_inputs(seed: int = 0) -> dict:
    key = jax.random.key(seed)
    ks = jax.random.split(key, 24)
    f32 = jnp.float32

    def nrm(k, shape, scale):
        return jax.random.normal(k, shape, f32) * scale

    def gain(k, shape):
        return 1.0 + 0.02 * jax.random.normal(k, shape, f32)

    return {
        'x': nrm(ks[0], (BATCH, SEQ, D_MODEL), 1.0),
        'meta_tokens': nrm(ks[1], (N_META, D_MODEL), 1.0),
        'g_mix': gain(ks[2], (DEPTH, D_MODEL)),
        'w_in': nrm(ks[3], (DEPTH, D_MODEL, IN_WIDTH), D_MODEL ** -0.5),
        'lambda_q1': nrm(ks[4], (DEPTH, A_HEAD_DIM), 0.1),
        'lambda_k1': nrm(ks[5], (DEPTH, A_HEAD_DIM), 0.1),
        'lambda_q2': nrm(ks[6], (DEPTH, A_HEAD_DIM), 0.1),
        'lambda_k2': nrm(ks[7], (DEPTH, A_HEAD_DIM), 0.1),
        'g_subln': gain(ks[8], (DEPTH, 2 * A_HEAD_DIM)),
        'g_qnorm': gain(ks[9], (DEPTH, B_HEAD_DIM)),
        'g_knorm': gain(ks[10], (DEPTH, B_HEAD_DIM)),
        'w_branch_a': nrm(ks[11], (DEPTH, A_V_WIDTH, D_MODEL), A_V_WIDTH ** -0.5),
        'w_branch_b': nrm(ks[12], (DEPTH, B_Q_WIDTH, D_MODEL), B_Q_WIDTH ** -0.5),
        'w_out': nrm(ks[13], (DEPTH, D_MODEL, D_MODEL), D_MODEL ** -0.5),
        'g_ffn': gain(ks[14], (DEPTH, D_MODEL)),
        'w_router': nrm(ks[15], (DEPTH, D_MODEL, N_EXPERTS), D_MODEL ** -0.5),
        'w_gate': nrm(ks[16], (DEPTH, N_EXPERTS, D_MODEL, EXPERT_FF), D_MODEL ** -0.5),
        'w_up': nrm(ks[17], (DEPTH, N_EXPERTS, D_MODEL, EXPERT_FF), D_MODEL ** -0.5),
        'w_down': nrm(ks[18], (DEPTH, N_EXPERTS, EXPERT_FF, D_MODEL), EXPERT_FF ** -0.5),
        'g_final': gain(ks[19], (D_MODEL,)),
    }

def second_block(x, meta_tokens, g_mix, w_in, lambda_q1, lambda_k1, lambda_q2, lambda_k2,
              g_subln, g_qnorm, g_knorm, w_branch_a, w_branch_b, w_out, g_ffn,
              w_router, w_gate, w_up, w_down, g_final):
    b = x.shape[0]
    meta = jnp.broadcast_to(meta_tokens[None].astype(x.dtype), (b, N_META, x.shape[-1]))
    h = jnp.concatenate([meta, x], axis=1)
    L = h.shape[1]
    pos = jnp.arange(L, dtype=jnp.int32)
    ang_row, ang_col = axial_angles(L)
    slopes = alibi_slopes(A_HEADS)
    cut = list(np.cumsum(SPLITS)[:-1])

    for layer in range(DEPTH):
        u = rms_norm_2(h, g_mix[layer])
        z = jnp.einsum('bld,df->blf', u, w_in[layer])
        qa, ka, va, qb, kb, vb, ga, gb = jnp.split(z, cut, axis=-1)

        lam_init = 0.8 - 0.6 * math.exp(-0.3 * layer)
        lam = (jnp.exp(jnp.sum(lambda_q1[layer].astype(jnp.float32) * lambda_k1[layer].astype(jnp.float32)))
               - jnp.exp(jnp.sum(lambda_q2[layer].astype(jnp.float32) * lambda_k2[layer].astype(jnp.float32)))
               + lam_init)
        oa = diff_attention(qa.reshape(b, L, A_HEADS, 2, A_HEAD_DIM),
                            ka.reshape(b, L, A_HEADS, 2, A_HEAD_DIM),
                            va.reshape(b, L, A_HEADS, 2 * A_HEAD_DIM), pos, slopes, lam)
        oa = (rms_norm_2(oa, g_subln[layer]) * (1.0 - lam_init)).reshape(b, L, A_V_WIDTH)

        qh = axial_rope(rms_norm_2(qb.reshape(b, L, B_HEADS, B_HEAD_DIM), g_qnorm[layer]), ang_row, ang_col)
        kh = axial_rope(rms_norm_2(kb.reshape(b, L, B_KV_HEADS, B_HEAD_DIM), g_knorm[layer]), ang_row, ang_col)
        ob = gqa_attention(qh.reshape(b, L, B_KV_HEADS, B_GROUP, B_HEAD_DIM), kh,
                           vb.reshape(b, L, B_KV_HEADS, B_HEAD_DIM)).reshape(b, L, B_Q_WIDTH)

        ya = jnp.einsum('blf,fd->bld', oa, w_branch_a[layer])
        yb = jnp.einsum('blf,fd->bld', ob, w_branch_b[layer])
        merged = jax.nn.sigmoid(ga) * ya + jax.nn.sigmoid(gb) * yb
        h = h + jnp.einsum('bld,de->ble', merged, w_out[layer])

        h = h + expert_choice_ffn(rms_norm_2(h, g_ffn[layer]), w_router[layer], w_gate[layer],
                                  w_up[layer], w_down[layer])

    return rms_norm_2(h, g_final)[:, N_META:]


def setup_inputs(seed=0):
    out = dict(first_inputs(seed))
    for name, value in second_inputs(seed + 1).items():
        if name != "x":
            out[name + "_2"] = value
    return out


def reference(
    x, c, ctx, c_ctx, ada_w, ada_b, norm1_g, norm2_g, w_in, rwkv_conv_w, decay_w0, decay_w2,
    iclr_a0, iclr_a2, gate_g2, k_k, k_a, r_k, gn_g, gn_b, fourier_g, w_out, ffn_w_up,
    ffn_conv_w, ffn_conv_b, ffn_w_down, final_g, meta_tokens_2, g_mix_2, w_in_2, lambda_q1_2,
    lambda_k1_2, lambda_q2_2, lambda_k2_2, g_subln_2, g_qnorm_2, g_knorm_2, w_branch_a_2,
    w_branch_b_2, w_out_2, g_ffn_2, w_router_2, w_gate_2, w_up_2, w_down_2, g_final_2,
):
    x = first_block(
        x, c, ctx, c_ctx, ada_w, ada_b, norm1_g, norm2_g, w_in, rwkv_conv_w, decay_w0, decay_w2,
        iclr_a0, iclr_a2, gate_g2, k_k, k_a, r_k, gn_g, gn_b, fourier_g, w_out, ffn_w_up,
        ffn_conv_w, ffn_conv_b, ffn_w_down, final_g,
    )
    return second_block(
        x, meta_tokens_2, g_mix_2, w_in_2, lambda_q1_2, lambda_k1_2, lambda_q2_2, lambda_k2_2,
        g_subln_2, g_qnorm_2, g_knorm_2, w_branch_a_2, w_branch_b_2, w_out_2, g_ffn_2,
        w_router_2, w_gate_2, w_up_2, w_down_2, g_final_2,
    )


_drawn_inputs = setup_inputs


def setup_inputs(seed=0):
    import zlib

    import numpy as np

    out = dict(_drawn_inputs(seed))
    spreads = {}
    factors = {'c_ctx': 2.788,
     'decay_w2': 8.0,
     'iclr_a2': 4.795,
     'k_k': 5.703,
     'k_a': 3.854,
     'gn_g': 5.808,
     'gn_b': 6.207,
     'fourier_g': 3.351,
     'ffn_conv_b': 4.426,
     'g_mix_2': 2.984,
     'lambda_q1_2': 8.0,
     'lambda_k1_2': 2.685,
     'g_subln_2': 4.588,
     'g_qnorm_2': 8.0,
     'g_knorm_2': 8.0,
     'g_ffn_2': 3.752}
    for name, (base, spread) in spreads.items():
        noise = np.random.default_rng([zlib.crc32(name.encode()), seed]).standard_normal(out[name].shape)
        drawn = base * np.exp(spread * noise) if base else spread * noise
        out[name] = jnp.asarray(drawn.astype(out[name].dtype))
    for name, factor in factors.items():
        out[name] = (out[name] * factor).astype(out[name].dtype)
    return out
```

```python
from contextlib import ExitStack
import math

import numpy as np

import concourse.bass as bass
from concourse import mybir

ALU = mybir.AluOpType
ACT = mybir.ActivationFunctionType
AX = mybir.AxisListType.X
F32 = mybir.dt.float32
P = 128

D = 1024
KD = D // P
TX = 256
TC = 256
TB = TX + TC
FW = 512
RW = 512
HEAD = 64
NJ = RW // P
C = 64
DFF = 2816
NG = DFF // P
GRID = 64
ROWS = TX // GRID
EPS = 1e-6
GN_EPS = 64e-5
KK_EPS = 1e-12
LOG_DECAY = math.exp(-0.5)

META = 16
L = META + TX
QC = ((0, 128), (128, 128), (256, 16))
AH = 8
BH = 8
NE = 16
EFF = 512
CAP = 2 * L // NE
SLOTS = 64
LAM_INIT = 0.8 - 0.6

W_ADA, W_IN, W_OUT, W_UP, W_DOWN, W_IN2, W_A, W_B, W_OUT2, W_END = 0, 12, 17, 19, 30, 36, 49, 51, 53, 55
RING = 4
WBLK = 4096


def block_columns(b):
    return 384 if b == W_OUT - 1 else 512


def block_rows(b):
    return 6 if b in (W_DOWN + 2, W_DOWN + 5) else 8


def constant_tables():
    t = {}
    i = np.arange(P)
    t["ident"] = np.eye(P)
    t["ones"] = np.ones((P, P))
    t["headones"] = (i[:, None] // 64 == i[None, :] // 64).astype(float)
    t["sign"] = np.where(i < 64, 1.0, -1.0)[:, None]
    a, b = i[:, None], i[None, :]
    same_head = a // 64 == b // 64
    same_8 = a // 8 == b // 8
    for d in range(2):
        before = (a < b) if d == 0 else (a > b)
        after = (a > b) if d == 0 else (a < b)
        t[f"diagT{d}"] = -1.0 * (same_head & same_8 & before)
        t[f"offT{d}"] = -1.0 * (same_head & ~same_8 & before)
        t[f"diag{d}"] = -1.0 * (same_head & same_8 & after)
        ra, cb = a % 64, b % 64
        strict = (ra < cb) if d == 0 else (ra > cb)
        incl = strict | (ra == cb)
        t[f"gram{d}"] = np.where(b < 64, strict, incl) * np.where(a < 64, 1.0, -1.0)
        tok = np.arange(TB) % C
        t[f"keep{d}"] = np.tile((tok != (0 if d == 0 else C - 1)).astype(float), (P, 1))
    g = FW // 8
    cc = np.arange(g)
    ang = 2 * np.pi * np.outer(cc, cc) / g
    for name, f in (("chan_cos", np.cos), ("chan_sin", np.sin)):
        m = np.zeros((P, P))
        m[:64, :64] = m[64:, 64:] = f(ang)
        t[name] = m
    tt = np.arange(TX)
    ang = 2 * np.pi * (np.outer(tt, tt) % TX) / TX
    scale = 1.0 / math.sqrt(TX * g)
    for k in range(2):
        t[f"tok_cos{k}"] = np.cos(ang)[k * P:(k + 1) * P] * scale
        t[f"tok_sin{k}"] = -np.sin(ang)[k * P:(k + 1) * P] * scale
    rot = np.zeros((P, P))
    half, quarter = 64, 32
    for base in (0, half):
        for m in range(quarter):
            rot[base + quarter + m, base + m] = -1.0
            rot[base + m, base + quarter + m] = 1.0
    t["rotate"] = rot
    inv = (np.float32(10000.0) ** (-np.arange(0, half, 2, dtype=np.float32) / np.float32(half))).astype(np.float32)
    n = np.arange(TX)
    row = np.concatenate([np.zeros(META), n // GRID]).astype(np.float32)
    col = np.concatenate([np.zeros(META), n % GRID]).astype(np.float32)
    ang = np.concatenate([np.tile((inv[:, None] * row[None, :]), (2, 1)),
                          np.tile((inv[:, None] * col[None, :]), (2, 1))]).astype(np.float32)
    t["rope_cos"] = np.cos(ang)
    t["rope_sin"] = np.sin(ang)
    pos = np.arange(L)
    dist = np.abs(pos[:, None] - pos[None, :]).astype(float)
    dist[:META, :] = 0
    dist[:, :META] = 0
    for k, (q0, nq) in enumerate(QC):
        m = np.zeros((P, L))
        m[:nq] = dist[q0:q0 + nq]
        t[f"dist{k}"] = m
    t["slot"] = np.tile(np.arange(1, SLOTS + 1, dtype=float), (P, 1))
    return t


def placed(names_and_widths):
    at, out = 0, {}
    for n, w in names_and_widths:
        out[n] = (at, w)
        at += w
    return out, at


LATE = ("rotate", "rope_cos", "rope_sin", "dist0", "dist1", "dist2", "slot")
_widths = [(n, v.shape[1]) for n, v in constant_tables().items()]
CONST, NCONST = placed([x for x in _widths if x[0] not in LATE])
CONST2, NCONST2 = placed([x for x in _widths if x[0] in LATE])

PARAM_SIZES = [("ada_b", 48), ("norm1_g", 8), ("norm2_g", 8), ("conv", 36), ("w0", 8), ("a0", 8), ("k_k", 4),
               ("k_a", 4), ("r_k", 4), ("gn_g", 4), ("gn_b", 4), ("fourier_g", 4), ("ffn_conv", 9 * 44),
               ("ffn_b", 44), ("final_g", 8), ("g_mix", 8), ("subln", 1), ("qnorm", 1), ("knorm", 1),
               ("g_ffn", 8), ("g_final", 8)]
PARAM = {}
_at = 0
for _n, _c in PARAM_SIZES:
    PARAM[_n] = _at
    _at += _c
NPARAM = _at


class Places:

    def __init__(self, tensor, start, end):
        self.tensor, self.at, self.end = tensor, start, end

    def take(self, *shape):
        n = int(np.prod(shape))
        v = self.tensor[:, self.at:self.at + n]
        self.at += n
        assert self.at <= self.end, (self.at, self.end)
        if len(shape) == 2:
            return v.rearrange("p (a b) -> p a b", a=shape[0])
        if len(shape) == 3:
            return v.rearrange("p (a b c) -> p a b c", a=shape[0], b=shape[1])
        if len(shape) == 4:
            return v.rearrange("p (a b c d) -> p a b c d", a=shape[0], b=shape[1], c=shape[2])
        return v


class Tally:

    def __init__(self, sem, start=0):
        self.sem, self.n = sem, start

    def __call__(self, instruction):
        instruction.then_inc(self.sem, 1)
        self.n = self.n + 1

    def wait(self, engine):
        engine.wait_ge(self.sem, self.n)


class Unit:

    def __init__(self, diff, head, tile, first_map, out_head):
        self.diff, self.head, self.tile = diff, head, tile
        self.maps = 1 if diff else 2
        self.first_map, self.out_head = first_map, out_head


def attention_units():
    out = [Unit(True, hd, t, 3 * hd + t, hd) for hd in range(AH) for t in range(3)]
    n = len(out)
    for hd in range(0, BH, 2):
        for t in range(3):
            out.append(Unit(False, hd, t, n, AH + hd))
            n += 2
    return out


def two_blocks(nc, dram, out):
    with ExitStack() as ctx:
        mem = ctx.enter_context(nc.sbuf_tensor("mem", [P, (nc.sbuf_usable_end - nc.sbuf_base) // 64 * 16 - 16], F32))
        ps = ctx.enter_context(nc.psum_tensor("ps", [P, 8, 512], F32))
        sems = {}

        def S(name):
            if name not in sems:
                sems[name] = ctx.enter_context(nc.semaphore(name))
            return sems[name]

        def bank(b):
            return ps[:, b, :]

        total = mem.shape[1]
        whole = Places(mem, 0, total)
        ring_at = whole.at
        ring = [whole.take(WBLK) for _ in range(RING)]
        consts = whole.take(NCONST)
        params = whole.take(NPARAM)
        mod = whole.take(48, 2)
        coef1 = whole.take(KD, 2)
        coef2 = whole.take(KD)
        cond = whole.take(KD, 2)
        cond_act = whole.take(KD, 2)
        ka_rest = whole.take(NJ)
        ka_rest2 = whole.take(NJ)
        tokens = whole.take(KD, TB)
        xres = tokens[:, :, TC:TB]
        arena = whole.at

        def cst(name):
            a, n = CONST[name]
            return consts[:, a:a + n]

        def prm(name, i=0, n=1):
            return params[:, PARAM[name] + i:PARAM[name] + i + n]

        ident = cst("ident")

        m1 = Places(mem, arena, total)
        h = m1.take(KD, TB)
        squares = m1.take(KD, TB)
        r = m1.take(NJ, TX)
        k = m1.take(NJ, TB)
        v = m1.take(NJ, TB)
        kk = m1.take(NJ, TB)
        four = m1.take(NJ, TX)
        cum = m1.take(2, NJ, TB)
        wd = m1.take(TB)
        ad = m1.take(TB)
        gd = m1.take(TX)
        y = m1.take(2, NJ, TX)
        root = m1.take(TB)
        rstd = m1.take(TB)
        gate_w = m1.take(RW)
        at_h = Places(mem, arena, total)
        cum_before = at_h.take(2, NJ, TB)
        iclr = at_h.take(2, NJ, TB)
        at_cum = Places(mem, 16384 + arena, total)
        assert at_cum.at == arena + 2 * KD * TB + NJ * TX + 3 * NJ * TB + NJ * TX
        spectrum = at_cum.take(2, NJ, 2 * P)
        mod_rows = at_cum.take(2, 512)
        at_y = Places(mem, at_cum.at + 1024 + 512 + 512 + 256, total)
        decay_w = at_y.take(RW)
        iclr_w = at_y.take(RW)
        kk_sq = at_y.take(2, TB)

        ms = Places(mem, ring_at, ring_at + RING * WBLK)
        KB = [ms.take(NJ, 2, C) for _ in range(2)]
        KR = [ms.take(NJ, 2, C) for _ in range(2)]
        V0 = [ms.take(NJ, C) for _ in range(2)]
        EC = [ms.take(NJ, C) for _ in range(2)]
        EP = [ms.take(NJ, C) for _ in range(2)]
        EI = [ms.take(NJ, C) for _ in range(2)]
        T0 = [ms.take(NJ, C) for _ in range(2)]
        T1 = [ms.take(NJ, C) for _ in range(2)]
        GM = [ms.take(2, NJ, P) for _ in range(2)]
        VU = [ms.take(NJ, P) for _ in range(2)]
        KBT = [ms.take(NJ, P) for _ in range(2)]
        X = [ms.take(NJ, C) for _ in range(2)]
        Q = [ms.take(NJ, P) for _ in range(2)]
        B1, B2, B3, B4, B5 = ([ms.take(NJ, P) for _ in range(2)] for _ in range(5))

        ST = [x.rearrange("p (j c) -> p j c", j=NJ) for x in (root, rstd)]
        EW = [x.rearrange("p (j c) -> p j c", j=NJ) for x in (wd, ad)]

        mp = Places(mem, arena + 16384, total)
        rw = mp.take(NJ, TX)
        bonus = mp.take(NJ, TX)
        ysq = mp.take(NJ, TX)
        t4 = mp.take(NJ, TX)
        mf = Places(mem, arena, total)
        h2 = mf.take(KD, TX)
        sq2 = mf.take(KD, TX)
        g = mf.take(NG, TX)
        acc = mf.take(2, TX)

        squares_f = spectrum.rearrange("p a b c -> p (a b c)")[:, 0:NJ * TX].rearrange("p (k t) -> p k t", k=NJ)

        m2 = Places(mem, arena, total)
        H = m2.take(KD, L)
        u = m2.take(KD, L)
        late = m2.take(NCONST2)
        lam_s = m2.take(8)
        sub_gain = m2.take(1)
        rt2 = m2.take(L)
        rs2 = m2.take(L)
        sqq = [m2.take(L) for _ in range(2)]
        lam4 = Places(mem, m2.at - 2 * L, total).take(4, 64)
        expert_at = m2.at
        qa = m2.take(AH, L)
        ka = m2.take(AH, L)
        va = m2.take(AH, L)
        qb = m2.take(BH, L)
        kb = m2.take(2, L)
        vb = m2.take(2, L)
        ga = m2.take(KD, L)
        gb = m2.take(KD, L)
        V = m2.take(3, 10, P)
        oa, ob = va, ka
        sqV = V.rearrange("p a b c -> p (a b c)")[:, 0:KD * L].rearrange("p (k t) -> p k t", k=KD)
        mx = Places(mem, arena - KD * TB, arena)
        sc = [mx.take(2, L) for _ in range(2)]
        ee = [mx.take(2, L) for _ in range(2)]
        WT = [mx.take(3, L) for _ in range(2)]
        stat = [mx.take(8) for _ in range(2)]
        units = attention_units()

        def cst2(name):
            a, n = CONST2[name]
            return late[:, a:a + n]

        me = Places(mem, expert_at, total)
        utok = me.take(3, D)
        sel = me.take(3, NE, SLOTS)
        xring = [me.take(WBLK) for _ in range(2)]
        selT = me.take(NE // 2, L)
        xsT = me.take(KD, P)
        hid = me.take(EFF)
        hidT = me.take(EFF // P, P)
        yexp = me.take(D)
        eslots = ring + xring
        sqq8 = utok.rearrange("p t d -> p (t d)")[:, 0:KD * L].rearrange("p (k t) -> p k t", k=KD)
        mt = Places(mem, expert_at + 3 * D + 3 * NE * SLOTS + 2 * WBLK, total)
        aff_e, left, above, equal, places = (mt.take(L) for _ in range(5))
        sg = Places(mem, arena - KD * TB, arena)
        selA = sg.take(3, NE, SLOTS)
        router = sg.take(KD, NE)
        hgate = sg.take(EFF)
        logit = sg.take(3, NE)
        aff = sg.take(3, NE)
        placeT = sg.take(3, NE)
        rstat = sg.take(8)
        top8 = sg.take(8)
        counts = sg.take(2)

        last_use = {}
        for n in range(W_IN):
            last_use[n] = ("mod_rows", n + 1)
        dense = {"proj": (W_IN, W_OUT), "wout": (W_OUT, W_UP), "up": (W_UP, W_DOWN), "proj2": (W_IN2, W_A),
                 "branch_a": (W_A, W_B), "branch_b": (W_B, W_OUT2), "wout2": (W_OUT2, W_END)}
        for name, (b0, b1) in dense.items():
            n = 0
            for b in range(b0, b1):
                n += block_columns(b) // P
                last_use[b] = (name, n)
        for n in range(6):
            last_use[W_DOWN + n] = ("down_read", n + 1)
        use = {b: S("ring%d" % (b % RING)) for b in range(RING)}

        def load_block(sp, b, free=True):
            if b >= RING and free:
                sp.wait_ge(S(last_use[b - RING][0]), last_use[b - RING][1])
            n = block_rows(b) * block_columns(b)
            sp.dma_start(ring[b % RING][:, 0:n], dram["weights"][b, :, 0:n]).then_inc(use[b % RING], 16)

        def have_block(engine, b):
            engine.wait_ge(use[b % RING], 16 * (b // RING + 1))

        def block_view(b):
            n = block_rows(b) * block_columns(b)
            return ring[b % RING][:, 0:n].rearrange("p (k c) -> p k c", k=block_rows(b))

        block = ctx.enter_context(nc.Block())

        NORMS = {"norm1": (0, 0), "four": (1, 8), "norm2": (2, 12), "final1": (3, 20), "gmix": (4, 28),
                 "gffn": (5, 36), "last": (6, 44)}
        HEAD_NORMS = {"qk": 0, "oa": 10}

        def norm_root(name):
            return S("norm_roots"), NORMS[name][0] + 1

        JOBS = {"tiles_made": ("gram0", "gram1", "removals", "keys_turned", "values_turned", "A2",
                               "A2T", "A4", "Q1", "Q2", "inverse8", "M",
                               "MT", "M2", "M2T", "R1", "M4", "R2",
                               "R3", "held", "removed", "state_made"),
                "kept_by_scalar": ("keys_kept", "values_kept", "A2_kept", "A2T_kept", "A4_kept", "inverse8_kept",
                               "M_kept", "MT_kept", "M2_kept", "M2T_kept", "M4_kept", "held_kept",
                               "removed_kept"),
                "kept_by_vector": ("gram0_kept", "gram1_kept", "A_kept", "Q0_kept", "Q1_kept", "Q2_kept",
                               "R1_kept", "R2_kept", "R3_kept")}

        def turns_of(name):
            return S([k for k, jobs in JOBS.items() if name in jobs][0])

        def turn(name, s, d):
            jobs = [jobs for jobs in JOBS.values() if name in jobs][0]
            return turns_of(name), s * (2 * len(jobs)) + (2 * jobs.index(name) + d + 1)

        def free_bank(engine, name, n, banks=4):
            if n >= banks:
                engine.wait_ge(S(name + "_taken"), n - banks + 1)

        def proj_taken(engine, j):
            if j < 4:
                engine.wait_ge(S("proj_taken"), j + 1)
            elif j < 16:
                engine.wait_ge(S("conv_steps"), 2 * (j - 3))
            else:
                engine.wait_ge(S("proj_taken"), j - 11)

        @block.sync
        def _(sp):
            sp.dma_start(cond, dram["cond"]).then_inc(S("cond_in"), 16)
            sp.dma_start(tokens, dram["tokens"]).then_inc(S("tokens_in"), 16)
            sp.dma_start(consts, dram["consts"]).then_inc(S("consts_in"), 16)
            for b in range(0, W_OUT):
                load_block(sp, b)
            sp.wait_ge(S("state_kept"), 4 * 8)
            sp.wait_ge(S("y_kept"), 2 * 4)
            for b in range(W_OUT, W_END):
                load_block(sp, b, free=b >= W_OUT + RING)
            for s in range(6):
                if s < 4:
                    b = W_END - RING + (s - W_END % RING) % RING
                    sp.wait_ge(S(last_use[b][0]), last_use[b][1])
                else:
                    sp.wait_ge(S("gffn_norm"), KD)
                sp.dma_start(eslots[s], dram["experts"][s, :, :]).then_inc(S("eslot%d" % s), 16)
            with sp.Fori(1, NE // 2) as i:
                for s in range(6):
                    sp.wait_ge(S(("gate", "up_e", "down_e")[s // 2]), i * (2 if s >= 4 else 1))
                    sp.dma_start(eslots[s], dram["experts"][bass.ds(i * 6 + s, 1), :, :]
                                 .rearrange("o p n -> (o p) n")).then_inc(S("eslot%d" % s), 16)
            sp.wait_ge(S("out_ready"), KD)
            sp.dma_start(out, H[:, :, META:L]).then_inc(S("out_written"), 16)
            sp.wait_ge(S("out_written"), 16)

        @block.tensor
        def _(pe):
            mm = nc.tensor.matmul

            def norm_sums(name, sq, chunks, n, b):
                for c in range(chunks):
                    pe.wait_ge(S("norm_squares"), NORMS[name][1] + c + 1)
                    last = mm(bank(b)[:, 0:n], cst("ones"), sq[:, c, 0:n], start=c == 0, stop=c == chunks - 1)
                last.then_inc(S("norm_sums"), 1)

            def dense_product(name, rhs, n, wait_rhs=None, banks=4, width=None, wait_bank=None):
                b0, b1 = dense[name]
                j = 0
                for b in range(b0, b1):
                    have_block(pe, b)
                    w = block_view(b)
                    for c in range(block_columns(b) // P):
                        if wait_bank:
                            if j >= banks:
                                wait_bank(pe, j - banks)
                        else:
                            free_bank(pe, name, j, banks)
                        nn, rr = width(j) if width else (n, rhs)
                        for kc in range(KD):
                            if j == 0 and wait_rhs:
                                wait_rhs(kc)
                            last = mm(bank(j % banks)[:, 0:nn], w[:, kc, c * P:(c + 1) * P], rr(kc),
                                      start=kc == 0, stop=kc == KD - 1)
                        last.then_inc(S(name), 1)
                        j += 1

            pe.wait_ge(S("consts_in"), 16)
            norm_sums("norm1", squares, KD, TB, 7)

            def turn_mod(n):
                pe.wait_ge(S("mod_rows_kept"), n + 1)
                for c in range(4):
                    i = 4 * n + c
                    last = nc.tensor.transpose(bank(2)[:, 2 * i:2 * i + 2], mod_rows[0:2, n % 2, c * P:(c + 1) * P],
                                               ident[0:2, 0:2])
                last.then_inc(S("mod_turned"), 1)

            pe.wait_ge(S("cond_act"), 1)
            for n in range(W_IN):
                have_block(pe, n)
                if n >= 2:
                    pe.wait_ge(S("mod_rows_kept"), n - 1)
                for kc in range(KD):
                    last = mm(bank(n % 2)[0:2, :], cond_act[:, kc, :], block_view(n)[:, kc, :],
                              start=kc == 0, stop=kc == KD - 1)
                last.then_inc(S("mod_rows"), 1)
                if n >= 1:
                    turn_mod(n - 1)
            turn_mod(W_IN - 1)

            pe.wait_ge(S("mod_kept"), 1)
            dense_product("proj", None, None,
                          wait_rhs=lambda kc: pe.wait_ge(S("h_ready"), 2 * (kc + 1)),
                          width=lambda j: ((TX, lambda kc: h[:, kc, TC:TB]) if j < 8 or j == 18
                                           else (TB, lambda kc: h[:, kc, :])),
                          wait_bank=proj_taken)

            pe.wait_ge(S("lora_in"), 32)
            pe.wait_ge(S("proj_taken"), 7)
            n = 0
            for w, src in ((decay_w, wd), (iclr_w, ad)):
                for d in range(2):
                    for j in range(NJ):
                        if n >= 2:
                            pe.wait_ge(S("lora_taken"), n - 1)
                        mm(bank(4 + n % 2), w[d * 64:d * 64 + 64, j * P:(j + 1) * P], src[d * 64:d * 64 + 64, :],
                           start=True, stop=True).then_inc(S("lora"), 1)
                        n += 1

            pe.wait_ge(*norm_root("norm1"))
            for t in range(2):
                for jj in range(2):
                    n = 2 * t + jj
                    if n >= 2:
                        pe.wait_ge(S("spectrum_kept"), n - 1)
                    for q in range(2):
                        j = 2 * jj + q
                        last = mm(bank(6 + n % 2)[:, q * 256:q * 256 + 256], four[:, j, t * P:(t + 1) * P],
                                  consts[:, CONST["chan_cos"][0]:CONST["chan_cos"][0] + 2 * P],
                                  start=True, stop=True)
                    last.then_inc(S("spectrum"), 1)
            for jj in range(2):
                pe.wait_ge(S("spectrum_kept"), 4)
                for q in range(2):
                    j = 2 * jj + q
                    i = 0
                    for t in range(2):
                        for part, table in ((0, "tok_cos%d"), (1, "tok_sin%d")):
                            last = mm(bank(6 + jj)[:, q * 256:q * 256 + 256], spectrum[:, t, j, part * P:(part + 1) * P],
                                      cst(table % t), start=i == 0, stop=i == 3)
                            i += 1
                last.then_inc(S("mixed"), 1)

            for j in range(NJ):
                pe.wait_ge(S("kk_squares"), j + 1)
                if j == 0:
                    pe.wait_ge(S("lora_taken"), 16)
                else:
                    pe.wait_ge(S("kk_root"), j)
                mm(bank(4), cst("headones"), kk_sq[:, j % 2, :], start=True, stop=True).then_inc(S("kk_sums"), 1)
            pe.wait_ge(S("mixed_kept"), 2)
            norm_sums("four", squares_f, NJ, TX, 6)
            pe.wait_ge(*norm_root("four"))
            pe.wait_ge(S("kk_root"), NJ)
            pe.wait_ge(S("state_zeroed"), 2)

            def B(d, i):
                return bank(4 * d + i)

            def steps(s, outputs):
                at = lambda d: 2 * s + d + 1
                cols = 2 * C if outputs else C
                for p in range(2):
                    for d in range(2):
                        if p == 0:
                            pe.wait_ge(S("keys_staged"), 7 * 2 * s + 7 * (d + 1))
                            pe.wait_ge(S("reads_staged"), at(d))
                            if outputs:
                                pe.wait_ge(S("outs_staged"), at(d) - 8)
                        for j in range(NJ):
                            hp = slice(64 * p, 64 * p + 64)
                            last = mm(B(d, p)[:, j * P:j * P + cols], KB[d][hp, j, :, :].rearrange("p a t -> p (a t)"),
                                      KR[d][hp, j, :, :].rearrange("p a t -> p (a t)")[:, 0:cols], start=True, stop=True)
                        last.then_inc(turns_of("gram%d" % p), 1)
                for d in range(2):
                    for j in range(NJ):
                        for p in range(2):
                            hp = slice(64 * p, 64 * p + 64)
                            mm(B(d, 2)[hp, j * P:j * P + 64], KB[d][hp, j, 1, :], KR[d][hp, j, 0, :], start=True, stop=True)
                            last = mm(B(d, 2)[hp, j * P + 64:j * P + P], KR[d][hp, j, 0, :], KB[d][hp, j, 1, :],
                                      start=True, stop=True)
                    last.then_inc(turns_of("removals"), 1)
                for d in range(2):
                    pe.wait_ge(*turn("gram0_kept", s, d))
                    for j in range(NJ):
                        last = nc.tensor.transpose(B(d, 3)[:, j * P:(j + 1) * P],
                                                   KB[d][:, j, :, :].rearrange("p a t -> p (a t)"), ident)
                    last.then_inc(turns_of("keys_turned"), 1)
                for d in range(2):
                    for j in range(NJ):
                        last = nc.tensor.transpose(B(d, 0)[0:64, j * P:(j + 1) * P], V0[d][:, j, :], ident)
                    last.then_inc(turns_of("values_turned"), 1)

                def pairs(name, b, lhs, rhs, *waits):
                    for d in range(2):
                        for w in waits:
                            pe.wait_ge(*turn(w, s, d))
                        for j in range(NJ):
                            last = mm(B(d, b)[:, j * P:(j + 1) * P], lhs[d][:, j, :], rhs[d][:, j, :], start=True, stop=True)
                        last.then_inc(turns_of(name), 1)

                pairs("A2", 1, B1, B2, "gram1_kept", "A_kept")
                pairs("A2T", 2, B2, B1)
                for d in range(2):
                    pe.wait_ge(*turn("A2_kept", s, d))
                    pe.wait_ge(*turn("A2T_kept", s, d))
                    pe.wait_ge(*turn("keys_kept", s, d))
                    for j in range(NJ):
                        last = mm(B(d, 3)[:, j * P:(j + 1) * P], B4[d][:, j, :], B3[d][:, j, :], start=True, stop=True)
                    last.then_inc(turns_of("A4"), 1)
                pairs("Q1", 0, B3, Q, "values_kept", "Q0_kept")
                pairs("Q2", 1, B1, Q, "A4_kept", "Q1_kept")
                for d in range(2):
                    pe.wait_ge(*turn("Q2_kept", s, d))
                    for j in range(NJ):
                        last = nc.tensor.transpose(B(d, 2)[:, j * P:(j + 1) * P], Q[d][:, j, :], ident)
                    last.then_inc(turns_of("inverse8"), 1)
                pairs("M", 3, B5, B2, "inverse8_kept")
                pairs("MT", 0, B2, B5)
                pairs("M2", 1, B4, B3, "M_kept", "MT_kept")
                pairs("M2T", 2, B3, B4)
                pairs("R1", 3, B3, Q)
                pairs("M4", 0, B5, B1, "M2_kept", "M2T_kept")
                pairs("R2", 1, B1, Q, "R1_kept")
                pairs("R3", 2, B2, Q, "M4_kept", "R2_kept")
                for d in range(2):
                    for j in range(NJ):
                        for p in range(2):
                            hp = slice(64 * p, 64 * p + 64)
                            o = B(d, 3)[hp, j * C:(j + 1) * C]
                            mm(o, KR[d][:, j, 0, :], ST[d][:, j, p * C:(p + 1) * C], start=True, stop=False)
                            last = mm(o, GM[d][0:64, p, j, 0:C], VU[d][0:64, j, p * C:(p + 1) * C], start=False, stop=True)
                    last.then_inc(turns_of("held"), 1)
                for d in range(2):
                    pe.wait_ge(*turn("R3_kept", s, d))
                    pe.wait_ge(*turn("held_kept", s, d))
                    for j in range(NJ):
                        for p in range(2):
                            last = mm(B(d, p)[64:128, j * C:(j + 1) * C], Q[d][:, j, p * C:(p + 1) * C], X[d][:, j, :],
                                      start=True, stop=True)
                    last.then_inc(turns_of("removed"), 1)
                if outputs:
                    for d in range(2):
                        pe.wait_ge(*turn("removed_kept", s, d))
                        for j in range(NJ):
                            for p in range(2):
                                hp = slice(64 * p, 64 * p + 64)
                                o = B(d, 3)[hp, j * C:(j + 1) * C]
                                mm(o, VU[d][:, j, p * C:(p + 1) * C], GM[d][:, p, j, C:2 * C], start=True, stop=False)
                                last = mm(o, ST[d][:, j, p * C:(p + 1) * C], KR[d][:, j, 1, :], start=False, stop=True)
                        last.then_inc(S("y_made"), 1)
                for d in range(2):
                    pe.wait_ge(*turn("removed_kept", s, d))
                    for j in range(NJ):
                        last = mm(B(d, 2)[:, j * P:(j + 1) * P], KBT[d][:, j, :], VU[d][:, j, :], start=True, stop=True)
                    last.then_inc(turns_of("state_made"), 1)
                pe.wait_ge(S("state_kept"), 4 * s + 4)
                if outputs:
                    pe.wait_ge(S("y_kept"), at(1) - 8)

            with pe.Fori(0, 4) as s:
                steps(s, False)
            with pe.Fori(4, 8) as s:
                steps(s, True)

            for j in range(NJ):
                pe.wait_ge(S("bonus_terms"), 6)
                mm(bank(j // 2)[:, (j % 2) * TX:(j % 2 + 1) * TX], cst("headones"), t4[:, j, :],
                   start=True, stop=True).then_inc(S("bonus_sums"), 1)
            pe.wait_ge(S("y_sum"), 1)
            for j in range(NJ):
                mm(bank(2 + j // 2)[:, (j % 2) * TX:(j % 2 + 1) * TX], cst("headones"), y[:, 0, j, :],
                   start=True, stop=True).then_inc(S("mean_sums"), 1)
            pe.wait_ge(S("gate_in"), 16)
            for j in range(NJ):
                mm(bank(4 + j // 2)[:, (j % 2) * TX:(j % 2 + 1) * TX], gate_w[:, j * P:(j + 1) * P], gd,
                   start=True, stop=True).then_inc(S("gates"), 1)
            pe.wait_ge(S("y_squares"), 1)
            for j in range(NJ):
                mm(bank(6 + j // 2)[:, (j % 2) * TX:(j % 2 + 1) * TX], cst("headones"), ysq[:, j, :],
                   start=True, stop=True).then_inc(S("var_sums"), 1)
            pe.wait_ge(S("rw_ready"), 1)
            dense_product("wout", lambda kc: four[:, kc, :] if kc < NJ else rw[:, kc - NJ, :], TX)

            norm_sums("norm2", sq2, KD, TX, 7)
            pe.wait_ge(S("wout_taken"), KD)
            dense_product("up", lambda kc: h2[:, kc, :], TX,
                          wait_rhs=lambda kc: pe.wait_ge(S("h2_ready"), kc + 1),
                          wait_bank=lambda e, j: e.wait_ge(S("ffn_taps"), 8 * (j + 1)))
            for half in range(2):
                for q in range(3):
                    b = W_DOWN + 3 * half + q
                    have_block(pe, b)
                    for c in range(4):
                        if q == 0 and half == 0:
                            pe.wait_ge(S("ffn_taps"), 8 * 2 * NG)
                            pe.wait_ge(S("ffn_mul"), NG)
                        for kc in range(block_rows(b)):
                            last = mm(bank(4 * half + c)[:, 0:TX], block_view(b)[:, kc, c * P:(c + 1) * P],
                                      g[:, 8 * q + kc, :], start=q == 0 and kc == 0,
                                      stop=q == 2 and kc == block_rows(b) - 1)
                        if q == 2 and c < 3:
                            last.then_inc(S("down"), 1)
                    last.then_inc(S("down_read"), 1)
            norm_sums("final1", sq2, KD, TX, 0)

            pe.wait_ge(S("consts2_in"), 16)
            norm_sums("gmix", sqV, KD, L, 7)
            dense_product("proj2", lambda kc: u[:, kc, :], L,
                          wait_rhs=lambda kc: pe.wait_ge(S("gmix_norm"), kc + 1))
            pe.wait_ge(S("proj2_taken"), 52)
            n = 0
            for e in range(10):
                if n >= 4:
                    pe.wait_ge(S("V_kept"), n - 3)
                src = va[:, e, :] if e < 8 else vb[:, e - 8, :]
                for t, (t0, nt) in enumerate(QC):
                    last = nc.tensor.transpose(bank(n % 4)[0:nt, t * P:(t + 1) * P], src[:, t0:t0 + nt], ident)
                last.then_inc(S("V_turned"), 1)
                n += 1
            for e in range(10):
                pe.wait_ge(S("head_squares"), e + 1)
                if e >= 1:
                    pe.wait_ge(S("head_roots"), e)
                mm(bank(4)[:, 0:L], cst("ones"), sqq[e % 2], start=True, stop=True).then_inc(S("head_sums"), 1)
            for e in range(10):
                pe.wait_ge(S("qk_normed"), e + 1)
                if e >= 2:
                    pe.wait_ge(S("qk_sined"), e - 1)
                src = qb[:, e, :] if e < 8 else kb[:, e - 8, :]
                mm(bank(5 + e % 2)[:, 0:L], cst2("rotate"), src, start=True, stop=True).then_inc(S("qk_turned"), 1)

            def scores(n):
                un = units[n]
                q0, nq = QC[un.tile]
                if n == 0:
                    pe.wait_ge(S("V_kept"), 10)
                if n == 24:
                    pe.wait_ge(S("qk_rotated"), 10)
                if n >= 2:
                    pe.wait_ge(S("scores_read"), n - 1)
                for m in range(2):
                    if un.diff:
                        a, b = qa[64 * m:64 * m + 64, un.head, q0:q0 + nq], ka[64 * m:64 * m + 64, un.head, :]
                    else:
                        a, b = qb[:, un.head + m, q0:q0 + nq], kb[:, un.head // 4, :]
                    last = mm(bank(2 * (n % 2) + m)[0:nq, 0:L], a, b, start=True, stop=True)
                last.then_inc(S("scores"), 1)

            def turn_weights(n):
                un = units[n]
                q0, nq = QC[un.tile]
                for m in range(un.maps):
                    w = un.first_map + m
                    pe.wait_ge(S("weights"), w + 1)
                    if w >= 2:
                        pe.wait_ge(S("weights_kept"), 2 * (w - 1))
                    elif w == 0:
                        pe.wait_ge(S("qk_rotated"), 10)
                    for t, (t0, nt) in enumerate(QC):
                        last = nc.tensor.transpose(bank(4 + w % 2)[0:nt, t * P:t * P + nq], ee[n % 2][0:nq, m, t0:t0 + nt],
                                                   ident[0:nq, 0:nq])
                    last.then_inc(S("weights_turned"), 1)

            def weigh_values(n):
                un = units[n]
                for m in range(un.maps):
                    hd = un.out_head + m
                    pe.wait_ge(S("weights_kept"), 2 * (un.first_map + m + 1))
                    if hd >= 2:
                        pe.wait_ge(S("attended_kept"), hd - 1)
                    e = un.head if un.diff else 8 + un.head // 4
                    for t, (t0, nt) in enumerate(QC):
                        last = mm(bank(6 + hd % 2)[:, 0:L], V[0:nt, t, e, :], WT[hd % 2][0:nt, t, :], start=t == 0,
                                  stop=t == 2)
                    last.then_inc(S("attended"), 1)

            for n in range(len(units) + 2):
                if n < len(units):
                    scores(n)
                if 1 <= n <= len(units):
                    turn_weights(n - 1)
                if n >= 2 and units[n - 2].tile == 2:
                    weigh_values(n - 2)
            for e in range(AH):
                pe.wait_ge(S("head_squares"), 10 + e + 1)
                if e >= 1:
                    pe.wait_ge(S("head_roots"), 10 + e)
                mm(bank(4)[:, 0:L], cst("ones"), sqq[e % 2], start=True, stop=True).then_inc(S("head_sums"), 1)
            pe.wait_ge(S("attended_kept"), 16)
            dense_product("branch_a", lambda kc: oa[:, kc, :], L,
                          wait_rhs=lambda kc: pe.wait_ge(S("oa_normed"), kc + 1))
            pe.wait_ge(S("branch_a_taken"), KD)
            dense_product("branch_b", lambda kc: ob[:, kc, :], L, wait_bank=lambda e, j: e.wait_ge(
                S("branch_b_steps"), 2 * (j + 1)))
            pe.wait_ge(S("branch_b_steps"), 2 * KD)
            dense_product("wout2", lambda kc: ga[:, kc, :], L)
            norm_sums("gffn", sqq8, KD, L, 7)
            pe.wait_ge(S("wout2_taken"), KD)

            pe.wait_ge(S("router_in"), 16)
            pe.wait_ge(S("gffn_norm"), KD)
            for t, (t0, nt) in enumerate(QC):
                for kc in range(KD):
                    last = mm(bank(0)[0:nt, t * NE:(t + 1) * NE], u[:, kc, t0:t0 + nt], router[:, kc, :],
                              start=kc == 0, stop=kc == KD - 1)
            last.then_inc(S("logits"), 1)
            for c in range(KD):
                if c >= 2:
                    pe.wait_ge(S("utok_kept"), c - 1)
                for t, (t0, nt) in enumerate(QC):
                    last = nc.tensor.transpose(bank(1 + c % 2)[0:nt, t * P:(t + 1) * P], u[:, c, t0:t0 + nt], ident)
                last.then_inc(S("u_turned"), 1)
            pe.wait_ge(S("aff"), 1)
            for t, (t0, nt) in enumerate(QC):
                last = nc.tensor.transpose(bank(3)[0:NE, t0:t0 + nt], aff[0:nt, t, :], ident[0:nt, 0:nt])
            last.then_inc(S("aff_turned"), 1)
            pe.wait_ge(S("places"), 1)
            for t, (t0, nt) in enumerate(QC):
                last = nc.tensor.transpose(bank(4)[0:nt, t * NE:(t + 1) * NE], places[0:NE, t0:t0 + nt],
                                           ident[0:NE, 0:NE])
            last.then_inc(S("places_turned"), 1)
            for i in range(NE // 2):
                pe.wait_ge(S("selA_ready"), 1)
                if i >= 2:
                    pe.wait_ge(S("selT_kept"), i - 1)
                for t, (t0, nt) in enumerate(QC):
                    last = nc.tensor.transpose(bank(5 + i % 2)[:, t0:t0 + nt],
                                               selA[0:nt, t, 2 * i:2 * i + 2, :].rearrange("p e s -> p (e s)"),
                                               ident[0:nt, 0:nt])
                last.then_inc(S("selT"), 1)
            pe.wait_ge(S("selT_kept"), NE // 2)
            pe.wait_ge(S("utok_kept"), KD)

            sel_flat = sel.rearrange("p t e s -> p t (e s)")

            def gather(i):
                for half in range(2):
                    for c in range(4):
                        for t, (t0, nt) in enumerate(QC):
                            last = mm(bank(half)[:, c * P:(c + 1) * P],
                                      utok[0:nt, t, (4 * half + c) * P:(4 * half + c + 1) * P],
                                      sel_flat[0:nt, t, bass.ds(i * P, P)], start=t == 0, stop=t == 2)
                    last.then_inc(S("gathered"), 1)

            def pair(i, more):
                pe.wait_ge(S("xs_kept"), 2 * i + 2)
                for name, b, s in (("gate", 2, 0), ("up_e", 3, 2)):
                    for e in range(2):
                        pe.wait_ge(S("eslot%d" % (s + e)), 16 * (i + 1))
                        w = eslots[s + e].rearrange("p (k c) -> p k c", k=KD)
                        for kc in range(KD):
                            last = mm(bank(b)[64 * e:64 * e + 64, :], xsT[:, kc, 64 * e:64 * e + 64], w[:, kc, :],
                                      start=kc == 0, stop=kc == KD - 1)
                    last.then_inc(S(name), 1)
                if more:
                    gather(i + 1)
                pe.wait_ge(S("hid"), i + 1)
                for f in range(4):
                    last = nc.tensor.transpose(bank(2)[:, f * P:(f + 1) * P], hid[:, f * P:(f + 1) * P], ident)
                last.then_inc(S("hid_turned"), 1)
                pe.wait_ge(S("hidT"), i + 1)
                for half in range(2):
                    for e in range(2):
                        pe.wait_ge(S("eslot%d" % (4 + e)), 16 * (i + 1))
                        w = eslots[4 + e].rearrange("p (k c) -> p k c", k=4)
                        for f in range(4):
                            last = mm(bank(4 + half)[64 * e:64 * e + 64, :], hidT[:, f, 64 * e:64 * e + 64],
                                      w[:, f, half * 512:(half + 1) * 512], start=f == 0, stop=f == 3)
                    last.then_inc(S("down_e"), 1)
                for c in range(KD):
                    pe.wait_ge(S("y_e"), 2 * i + 1 + c // 4)
                    if c >= 2:
                        pe.wait_ge(S("added"), i * KD + c - 1)
                    mm(bank(6 + c % 2)[:, 0:L], yexp[:, c * P:(c + 1) * P], selT[:, bass.ds(i, 1), :]
                       .rearrange("p o t -> p (o t)"), start=True, stop=True).then_inc(S("spread"), 1)
                pe.wait_ge(S("added"), i * KD + KD)

            gather(0)
            with pe.Fori(0, NE // 2 - 1) as i:
                pair(i, True)
            pair(NE // 2 - 1, False)
            norm_sums("last", sqq8, KD, L, 0)

        def token_at(s, d, outputs):
            return s * C if d == 0 else s * -C + ((TB + TC - C) if outputs else (TC - C))

        def bc(ap, *shape):
            return ap.to_broadcast(list(shape))

        def per_channel(cols, n, width):
            return bc(cols.rearrange("p (n o) -> p n o", o=1), P, n, width)

        def four_chunks(b):
            return ps[:, b:b + 2, :].rearrange("p b (q t) -> p (b q) t", q=2)

        def by_pair(b, width):
            return bank(b)[:, 0:NJ * width].rearrange("p (j c) -> p j c", j=NJ)

        @block.scalar
        def _(act):
            A = nc.scalar.activation
            act.dma_start(params, dram["params"]).then_inc(S("params_in"), 16)
            act.dma_start(decay_w, dram["decay_w2"]).then_inc(S("lora_in"), 16)
            act.dma_start(iclr_w, dram["iclr_a2"]).then_inc(S("lora_in"), 16)
            act.dma_start(gate_w, dram["gate_g2"]).then_inc(S("gate_in"), 16)

            def norm(name, src, sq, chunks, n, b, rt, eps, wait=None, width=D):
                for c in range(chunks):
                    if wait:
                        wait(c)
                    A(sq[:, c, 0:n], src[:, c, 0:n], ACT.Square).then_inc(S("norm_squares"), 1)
                act.wait_ge(S("norm_sums"), NORMS[name][0] + 1)
                A(rt[:, 0:n], bank(b)[:, 0:n], ACT.Sqrt, scale=1.0 / width, bias=eps).then_inc(S("norm_roots"), 1)

            act.wait_ge(S("cond_in"), 16)
            A(cond_act, cond, ACT.Silu).then_inc(S("cond_act"), 1)
            act.wait_ge(S("tokens_in"), 16)
            norm("norm1", tokens, squares, KD, TB, 7, root, EPS)
            for n in range(W_IN):
                act.wait_ge(S("mod_rows"), n + 1)
                if n >= 2:
                    act.wait_ge(S("mod_turned"), n - 1)
                A(mod_rows[0:2, n % 2, :], bank(n % 2)[0:2, :], ACT.Copy).then_inc(S("mod_rows_kept"), 1)
            for c in range(KD):
                for half in range(2):
                    act.wait_ge(S("h_scaled"), 2 * c + half + 1)
                    x = h[:, c, half * TC:(half + 1) * TC]
                    A(x, x, ACT.Identity, bias=mod[:, c, 1 - half:2 - half]).then_inc(S("h_ready"), 1)
            for j in range(19):
                act.wait_ge(S("proj"), j + 1)
                b = bank(j % 4)
                if j < 4:
                    A(four[:, j, :], b[:, 0:TX], ACT.Copy).then_inc(S("proj_taken"), 1)
                elif j < 16:
                    dst = r[:, j - 4, :] if j < 8 else k[:, j - 8, :] if j < 12 else v[:, j - 12, :]
                    n = TX if j < 8 else TB
                    A(dst, b[:, 0:n], ACT.Copy, scale=prm("conv", 12 + j - 4)).then_inc(S("conv_mid"), 1)
                elif j == 16:
                    A(wd, b, ACT.Tanh).then_inc(S("proj_taken"), 1)
                elif j == 17:
                    A(ad, b, ACT.Copy).then_inc(S("proj_taken"), 1)
                else:
                    A(gd, b[:, 0:TX], ACT.Sigmoid).then_inc(S("proj_taken"), 1)
            n = 0
            for dst, base in ((cum_before, "w0"), (iclr, "a0")):
                for d in range(2):
                    for j in range(NJ):
                        act.wait_ge(S("lora"), n + 1)
                        A(dst[:, d, j, :], bank(4 + n % 2), ACT.Sigmoid, bias=prm(base, NJ * d + j))\
                            .then_inc(S("lora_taken"), 1)
                        n += 1
            for n in range(4):
                act.wait_ge(S("spectrum"), n + 1)
                t, jj = n // 2, n % 2
                A(spectrum[:, t, 2 * jj:2 * jj + 2, :], bank(6 + n % 2).rearrange("p (q c) -> p q c", q=2), ACT.Copy)\
                    .then_inc(S("spectrum_kept"), 1)
            for jj in range(2):
                act.wait_ge(S("mixed"), jj + 1)
                A(four[:, 2 * jj:2 * jj + 2, :], bank(6 + jj).rearrange("p (q c) -> p q c", q=2), ACT.Copy)\
                    .then_inc(S("mixed_kept"), 1)
            for j in range(NJ + 1):
                if j < NJ:
                    act.wait_ge(S("kk_scaled"), j + 1)
                    if j >= 2:
                        act.wait_ge(S("kk_sums"), j - 1)
                    A(kk_sq[:, j % 2, :], kk[:, j, :], ACT.Square).then_inc(S("kk_squares"), 1)
                if j >= 1:
                    act.wait_ge(S("kk_sums"), j)
                    if j >= 2:
                        act.wait_ge(S("kk_recip"), j - 1)
                    A(root, bank(4), ACT.Sqrt, bias=KK_EPS).then_inc(S("kk_root"), 1)
            act.wait_ge(S("mixed_kept"), 2)
            act.wait_ge(S("kk_recip"), NJ)
            norm("four", four, squares_f, NJ, TX, 6, root, EPS, width=FW)

            def steps(s, outputs):
                at = lambda d: 2 * s + d + 1
                for d in range(2):
                    t = token_at(s, d, outputs)
                    A(EC[d], cum[:, d, :, bass.ds(t, C)], ACT.Exp, scale=-LOG_DECAY)
                    A(EP[d], cum_before[:, d, :, bass.ds(t, C)], ACT.Exp, scale=-LOG_DECAY)
                    A(EI[d], cum[:, d, :, bass.ds(t, C)], ACT.Exp, scale=LOG_DECAY).then_inc(S("decays"), 1)

                def keep(name, b, dst, *waits, scale=1.0):
                    for d in range(2):
                        act.wait_ge(*turn(name, s, d))
                        for w in waits:
                            act.wait_ge(*turn(w, s, d))
                        A(dst[d], by_pair(4 * d + b, P), ACT.Copy, scale=scale).then_inc(turns_of(name + "_kept"), 1)

                for d in range(2):
                    act.wait_ge(*turn("keys_turned", s, d))
                    A(KBT[d], by_pair(4 * d + 3, P), ACT.Copy, scale=cst("sign")).then_inc(turns_of("keys_kept"), 1)
                for d in range(2):
                    act.wait_ge(*turn("values_turned", s, d))
                    A(VU[d][0:64, :, :], by_pair(4 * d, P)[0:64, :, :], ACT.Copy).then_inc(turns_of("values_kept"), 1)
                keep("A2", 1, B3)
                keep("A2T", 2, B4)
                keep("A4", 3, B1, "Q0_kept")
                keep("inverse8", 2, B2)
                keep("M", 3, B3)
                keep("MT", 0, B4)
                keep("M2", 1, B1)
                keep("M2T", 2, B5)
                keep("M4", 0, B2)
                for d in range(2):
                    act.wait_ge(*turn("held", s, d))
                    A(X[d], by_pair(4 * d + 3, C), ACT.Copy).then_inc(turns_of("held_kept"), 1)
                for d in range(2):
                    act.wait_ge(*turn("removed", s, d))
                    A(VU[d][64:128, :, :].rearrange("p j (h c) -> p h j c", h=2),
                      ps[64:128, 4 * d:4 * d + 2, 0:NJ * C].rearrange("p h (j c) -> p h j c", j=NJ), ACT.Copy).then_inc(turns_of("removed_kept"), 1)
                if outputs:
                    for d in range(2):
                        act.wait_ge(S("y_made"), at(d) - 8)
                        t = s * C - TC if d == 0 else s * -C + (TB - C)
                        A(y[:, d, :, bass.ds(t, C)], by_pair(4 * d + 3, C), ACT.Copy).then_inc(S("y_kept"), 1)
                act.wait_ge(S("state_kept"), 4 * s + 4)

            act.wait_ge(S("sums_before"), 2)
            with act.Fori(0, 4) as s:
                steps(s, False)
            with act.Fori(4, 8) as s:
                steps(s, True)

            act.wait_ge(S("y_centred"), 1)
            A(ysq, y[:, 0, :, :], ACT.Square).then_inc(S("y_squares"), 1)
            act.wait_ge(S("var_sums"), NJ)
            A(y[:, 1, :, :], four_chunks(6), ACT.Sqrt, scale=1.0 / HEAD, bias=GN_EPS).then_inc(S("var_root"), 1)

            norm("norm2", xres, sq2, KD, TX, 7, root, EPS, wait=lambda c: act.wait_ge(S("wout_taken"), c + 1))
            for c in range(KD):
                act.wait_ge(S("h2_scaled"), c + 1)
                A(h2[:, c, :], h2[:, c, :], ACT.Identity, bias=mod[:, 24 + c, 0:1]).then_inc(S("h2_ready"), 1)

            def activate_gate(j):
                act.wait_ge(S("ffn_taps"), 8 * (j + 1))
                A(g[:, j, :], g[:, j, :], ACT.Silu).then_inc(S("ffn_act"), 1)

            for j in range(2 * NG):
                act.wait_ge(S("up"), j + 1)
                if j >= NG + 2:
                    act.wait_ge(S("ffn_mul"), j - NG - 1)
                dst = g[:, j, :] if j < NG else acc[:, j % 2, :]
                A(dst, bank(j % 4)[:, 0:TX], ACT.Identity, scale=prm("ffn_conv", 4 * 2 * NG + j),
                  bias=prm("ffn_b", j)).then_inc(S("ffn_mid"), 1)
                if 1 <= j <= NG:
                    activate_gate(j - 1)
            norm("final1", xres, sq2, KD, TX, 0, root, EPS, wait=lambda c: act.wait_ge(S("down_taken"), c + 1))

            norm("gmix", H, sqV, KD, L, 7, rt2, EPS,
                 wait=lambda c: (act.wait_ge(S("H_ready"), c + 1), act.wait_ge(S("meta_in"), 16)))
            for j in range(52):
                act.wait_ge(S("proj2"), j + 1)
                dst = (qa[:, j, :] if j < 8 else ka[:, j - 8, :] if j < 16 else va[:, j - 16, :] if j < 24
                       else qb[:, j - 24, :] if j < 32 else kb[:, j - 32, :] if j < 34 else vb[:, j - 34, :] if j < 36
                       else ga[:, j - 36, :] if j < 44 else gb[:, j - 44, :])
                A(dst, bank(j % 4)[:, 0:L], ACT.Sigmoid if j >= 36 else ACT.Copy).then_inc(S("proj2_taken"), 1)

            def head_norm(name, head, n, width=P):
                for e in range(n + 1):
                    if e < n:
                        if e >= 2:
                            act.wait_ge(S("head_sums"), HEAD_NORMS[name] + e - 1)
                        A(sqq[e % 2], head(e), ACT.Square).then_inc(S("head_squares"), 1)
                    if e >= 1:
                        act.wait_ge(S("head_sums"), HEAD_NORMS[name] + e)
                        if e >= 2:
                            act.wait_ge(S("head_recips"), HEAD_NORMS[name] + e - 1)
                        A(rt2, bank(4)[:, 0:L], ACT.Sqrt, scale=1.0 / width, bias=EPS).then_inc(S("head_roots"), 1)

            act.wait_ge(S("lam_sums"), 2)
            act.wait_ge(S("proj2_taken"), 52)
            head_norm("qk", lambda e: qb[:, e, :] if e < 8 else kb[:, e - 8, :], 10)
            A(lam_s[:, 2:4], lam_s[:, 0:2], ACT.Exp).then_inc(S("lam_exp"), 1)

            def exponentials(n):
                un = units[n]
                nq = QC[un.tile][1]
                act.wait_ge(S("maxima"), n + 1)
                if n >= 2:
                    p = units[n - 2]
                    act.wait_ge(S("weights_turned"), p.first_map + p.maps)
                scale = HEAD ** -0.5 if un.diff else P ** -0.5
                for m in range(2):
                    src = sc[n % 2][0:nq, m, :] if un.diff else bank(2 * (n % 2) + m)[0:nq, 0:L]
                    last = A(ee[n % 2][0:nq, m, :], src, ACT.Exp, scale=scale, bias=stat[n % 2][0:nq, 2 + m:3 + m],
                             accum_out=stat[n % 2][0:nq, 4 + m:5 + m])
                last.then_inc(S("scores_read"), 1)

            def keep_weights(n):
                un = units[n]
                q0, nq = QC[un.tile]
                for m in range(un.maps):
                    w = un.first_map + m
                    buf = WT[(un.out_head + m) % 2]
                    act.wait_ge(S("weights_turned"), w + 1)
                    if un.tile == 0 and un.out_head + m >= 2:
                        act.wait_ge(S("attended"), un.out_head + m - 1)
                    b = bank(4 + w % 2)
                    A(buf[:, 0:2, q0:q0 + nq], b[:, 0:2 * P].rearrange("p (t q) -> p t q", t=2)[:, :, 0:nq], ACT.Copy)\
                        .then_inc(S("weights_kept"), 1)
                    A(buf[0:16, 2, q0:q0 + nq], b[0:16, 2 * P:2 * P + nq], ACT.Copy).then_inc(S("weights_kept"), 1)

            def keep_attended(n):
                un = units[n]
                for m in range(un.maps):
                    hd = un.out_head + m
                    act.wait_ge(S("attended"), hd + 1)
                    dst = oa[:, hd, :] if un.diff else ob[:, hd - AH, :]
                    A(dst, bank(6 + hd % 2)[:, 0:L], ACT.Copy).then_inc(S("attended_kept"), 1)

            for n in range(len(units) + 2):
                if n < len(units):
                    exponentials(n)
                if 1 <= n <= len(units):
                    keep_weights(n - 1)
                if n >= 2 and units[n - 2].tile == 2:
                    keep_attended(n - 2)
            act.wait_ge(S("attended_kept"), 16)
            head_norm("oa", lambda e: oa[:, e, :], AH)
            norm("gffn", H, sqq8, KD, L, 7, rt2, EPS, wait=lambda c: act.wait_ge(S("wout2_taken"), c + 1))

            act.wait_ge(S("logits_shifted"), 2)
            for rows, t0, t1 in ((P, 0, 2), (16, 2, 3)):
                A(aff[0:rows, t0:t1, :], logit[0:rows, t0:t1, :], ACT.Exp).then_inc(S("logits_exp"), 1)
            for c in range(KD):
                act.wait_ge(S("u_turned"), c + 1)
                b = bank(1 + c % 2)
                A(utok[:, 0:2, c * P:(c + 1) * P], b[:, 0:2 * P].rearrange("p (t q) -> p t q", t=2), ACT.Copy)
                A(utok[0:16, 2, c * P:(c + 1) * P], b[0:16, 2 * P:3 * P], ACT.Copy).then_inc(S("utok_kept"), 1)
            for i in range(NE // 2):
                act.wait_ge(S("selT"), i + 1)
                act.wait_ge(S("places_turned"), 1)
                A(selT[:, i, :], bank(5 + i % 2)[:, 0:L], ACT.Copy).then_inc(S("selT_kept"), 1)

            def keep_gathered(i):
                for half in range(2):
                    act.wait_ge(S("gathered"), 2 * i + half + 1)
                    A(xsT[:, 4 * half:4 * half + 4, :], bank(half).rearrange("p (c s) -> p c s", c=4), ACT.Copy)\
                        .then_inc(S("xs_kept"), 1)

            def pair(i, more):
                act.wait_ge(S("gate"), i + 1)
                A(hgate, bank(2), ACT.Silu).then_inc(S("silu"), 1)
                if more:
                    act.wait_ge(S("up_e"), i + 1)
                    keep_gathered(i + 1)
                act.wait_ge(S("hid_turned"), i + 1)
                A(hidT, bank(2).rearrange("p (f s) -> p f s", f=4), ACT.Copy).then_inc(S("hidT"), 1)
                for half in range(2):
                    act.wait_ge(S("down_e"), 2 * i + half + 1)
                    A(yexp[:, half * 512:(half + 1) * 512], bank(4 + half), ACT.Copy).then_inc(S("y_e"), 1)
                act.wait_ge(S("hid"), i + 1)

            keep_gathered(0)
            with act.Fori(0, NE // 2 - 1) as i:
                pair(i, True)
            pair(NE // 2 - 1, False)
            norm("last", H, sqq8, KD, L, 0, rt2, EPS,
                 wait=lambda c: act.wait_ge(S("added"), NE // 2 * KD))

        @block.vector
        def _(dve):
            V_ = nc.vector
            tt, stt, ts = V_.tensor_tensor, V_.scalar_tensor_tensor, V_.tensor_scalar

            def apply_norm(name, src, dst, n, rt, rs, gain, done, chunks=KD):
                dve.wait_ge(*norm_root(name))
                V_.reciprocal(rs[:, 0:n], rt[:, 0:n]).then_inc(S("norm_recips"), 1)
                dve.wait_ge(S("norm_recips"), NORMS[name][0] + 1)
                for c in range(chunks):
                    stt(out=dst[:, c, :], in0=src[:, c, :], scalar=gain(c), in1=rs[:, 0:n], op0=ALU.mult,
                        op1=ALU.mult).then_inc(S(done), 1)

            dve.wait_ge(S("params_in"), 16)
            ts(ka_rest, prm("k_a", 0, NJ), -1.0, 1.0, ALU.mult, ALU.add)
            ts(ka_rest2, prm("k_a", 0, NJ), -2.0, 2.0, ALU.mult, ALU.add).then_inc(S("ka_rest"), 1)
            dve.wait_ge(*norm_root("norm1"))
            V_.reciprocal(rstd, root).then_inc(S("norm_recips"), 1)
            dve.wait_ge(S("mod_turned"), W_IN)
            tt(mod, bank(2)[:, 0:96].rearrange("p (n o) -> p n o", o=2), per_channel(prm("ada_b", 0, 48), 48, 2),
               ALU.add).then_inc(S("mod_kept"), 1)
            dve.wait_ge(S("mod_kept"), 1)
            stt(out=coef1, in0=mod[:, 8:16, :], scalar=1.0, in1=per_channel(prm("norm1_g", 0, KD), KD, 2),
                op0=ALU.add, op1=ALU.mult)
            stt(out=coef2, in0=mod[:, 32:40, 0], scalar=1.0, in1=prm("norm2_g", 0, KD), op0=ALU.add,
                op1=ALU.mult).then_inc(S("coefs"), 1)
            dve.wait_ge(S("coefs"), 1)
            dve.wait_ge(S("norm_recips"), 1)
            for c in range(KD):
                for half in range(2):
                    t = slice(half * TC, (half + 1) * TC)
                    stt(out=h[:, c, t], in0=tokens[:, c, t], scalar=coef1[:, c, 1 - half:2 - half], in1=rstd[:, t],
                        op0=ALU.mult, op1=ALU.mult).then_inc(S("h_scaled"), 1)
            for q in range(12):
                n_seq = 1 if q < 4 else 2
                dst = r[:, q, :] if q < 4 else k[:, q - 4, :] if q < 8 else v[:, q - 8, :]
                dst = dst.rearrange("p (n t) -> p n t", n=n_seq)
                src = bank((q + 4) % 4)[:, 0:n_seq * TX].rearrange("p (n t) -> p n t", n=n_seq)
                dve.wait_ge(S("conv_mid"), q + 1)
                stt(out=dst[:, :, 1:TX], in0=src[:, :, 0:TX - 1], scalar=prm("conv", q), in1=dst[:, :, 1:TX],
                    op0=ALU.mult, op1=ALU.add).then_inc(S("conv_steps"), 1)
                dve.wait_ge(S("conv_steps"), 2 * q + 1)
                stt(out=dst[:, :, 0:TX - 1], in0=src[:, :, 1:TX], scalar=prm("conv", 24 + q), in1=dst[:, :, 0:TX - 1],
                    op0=ALU.mult, op1=ALU.add).then_inc(S("conv_steps"), 1)
            dve.wait_ge(S("conv_steps"), 24)
            for j in range(NJ):
                ts(kk[:, j, :], k[:, j, :], prm("k_k", j), None, ALU.mult).then_inc(S("kk_scaled"), 1)
            for j in range(NJ):
                dve.wait_ge(S("kk_root"), j + 1)
                if j >= 1:
                    dve.wait_ge(S("kk_unit"), j)
                V_.reciprocal(rstd, root).then_inc(S("kk_recip"), 1)
                dve.wait_ge(S("kk_recip"), j + 1)
                tt(kk[:, j, :], kk[:, j, :], rstd, ALU.mult).then_inc(S("kk_unit"), 1)
            dve.wait_ge(S("kk_unit"), NJ)
            apply_norm("four", four, four, TX, root, rstd, lambda c: prm("fourier_g", c), "four_norm", NJ)
            for d in range(2):
                dve.wait_ge(S("lora_taken"), 16)
                for j in range(NJ):
                    x, o, keep = cum_before[:, d, j, :], cum[:, d, j, :], cst("keep%d" % d)
                    if d == 1:
                        x, o, keep = x[:, ::-1], o[:, ::-1], keep[:, ::-1]
                    last = V_.tensor_tensor_scan(o, keep, x, 0.0, ALU.mult, ALU.add)
                last.then_inc(S("sums"), 1)
            dve.wait_ge(S("proj"), 19)
            dve.wait_ge(S("four_norm"), NJ)
            for d in range(2):
                V_.memset(ST[d], 0.0).then_inc(S("state_zeroed"), 1)

            def steps(s, outputs):
                at = lambda d: 2 * s + d + 1
                cols = 2 * C if outputs else C
                for d in range(2):
                    t = token_at(s, d, outputs)
                    dve.wait_ge(S("decays"), at(d))
                    last_token = EC[d][:, :, C - 1:C] if d == 0 else EC[d][:, :, 0:1]
                    tt(EW[d], bc(last_token, P, NJ, P), bc(cst("headones").rearrange("p (o c) -> p o c", o=1), P, NJ, P),
                       ALU.mult)
                    tt(KR[d][:, :, 0, :], kk[:, :, bass.ds(t, C)], EP[d], ALU.mult).then_inc(S("reads_staged"), 1)
                    if outputs:
                        tt(KR[d][:, :, 1, :], r[:, :, bass.ds(t - TC, C)], EC[d], ALU.mult)\
                            .then_inc(S("outs_staged"), 1)
                for p in range(2):
                    for d in range(2):
                        dve.wait_ge(*turn("gram%d" % p, s, d))
                        mask = bc(cst("gram%d" % d)[:, 0:cols].rearrange("p (o c) -> p o c", o=1), P, NJ, cols)
                        tt(GM[d][:, p, :, 0:cols], by_pair(4 * d + p, P)[:, :, 0:cols], mask, ALU.mult)\
                            .then_inc(turns_of("gram%d_kept" % p), 1)
                for d in range(2):
                    dve.wait_ge(*turn("removals", s, d))
                    for dst, name, half in ((B1, "diagT%d", 0), (B5, "offT%d", 0), (B2, "diag%d", 1)):
                        src = bank(4 * d + 2).rearrange("p (j h o c) -> p j h o c", j=NJ, h=2, o=1)[:, :, half, :, :]
                        mask = cst(name % d).rearrange("p (o h c) -> p o h c", o=1, h=2)
                        last = tt(dst[d].rearrange("p j (h c) -> p j h c", h=2), bc(src, P, NJ, 2, C),
                                  bc(mask, P, NJ, 2, C), ALU.mult)
                    last.then_inc(turns_of("A_kept"), 1)
                for d in range(2):
                    dve.wait_ge(*turn("A_kept", s, d))
                    tt(Q[d], B1[d], bc(ident.rearrange("p (o c) -> p o c", o=1), P, NJ, P), ALU.add)\
                        .then_inc(turns_of("Q0_kept"), 1)
                before = "Q0_kept"
                for name, b in (("Q1", 0), ("Q2", 1), ("R1", 3), ("R2", 1), ("R3", 2)):
                    for d in range(2):
                        dve.wait_ge(*turn(name, s, d))
                        dve.wait_ge(*turn(before, s, d))
                        tt(Q[d], by_pair(4 * d + b, P), Q[d], ALU.add).then_inc(turns_of(name + "_kept"), 1)
                    before = name + "_kept"
                for d in range(2):
                    dve.wait_ge(*turn("state_made", s, d))
                    tt(ST[d], by_pair(4 * d + 2, P), ST[d], ALU.add).then_inc(S("state_kept"), 1)
                dve.wait_ge(S("state_kept"), 4 * s + 2)
                for d in range(2):
                    tt(ST[d], ST[d], EW[d], ALU.mult).then_inc(S("state_kept"), 1)

            with dve.Fori(0, 4) as s:
                steps(s, False)
            with dve.Fori(4, 8) as s:
                steps(s, True)

            n = Tally(S("mix_steps"))
            dve.wait_ge(S("y_kept"), 8)
            tt(y[:, 0, :, :], y[:, 0, :, :], y[:, 1, :, :], ALU.add).then_inc(S("y_sum"), 1)
            dve.wait_ge(S("mean_sums"), NJ)
            dve.wait_ge(S("y_sum"), 1)
            stt(out=y[:, 0, :, :], in0=four_chunks(2), scalar=-1.0 / HEAD, in1=y[:, 0, :, :], op0=ALU.mult,
                op1=ALU.add).then_inc(S("y_centred"), 1)
            dve.wait_ge(S("bonus_sums"), NJ)
            n(tt(bonus, four_chunks(0), v[:, :, TC:TB], ALU.mult))
            dve.wait_ge(S("var_root"), 1)
            n(V_.reciprocal(y[:, 1, :, :], y[:, 1, :, :]))
            n.wait(dve)
            n(tt(y[:, 0, :, :], y[:, 0, :, :], y[:, 1, :, :], ALU.mult))
            n.wait(dve)
            n(tt(y[:, 0, :, :], y[:, 0, :, :], per_channel(prm("gn_g", 0, NJ), NJ, TX), ALU.mult))
            n.wait(dve)
            n(tt(y[:, 0, :, :], y[:, 0, :, :], per_channel(prm("gn_b", 0, NJ), NJ, TX), ALU.add))
            n.wait(dve)
            n(tt(y[:, 0, :, :], y[:, 0, :, :], bonus, ALU.add))
            n.wait(dve)
            dve.wait_ge(S("gates"), NJ)
            tt(rw, four_chunks(4), y[:, 0, :, :], ALU.mult).then_inc(S("rw_ready"), 1)

            for c in range(KD):
                dve.wait_ge(S("wout"), c + 1)
                stt(out=xres[:, c, :], in0=bank(c % 4)[:, 0:TX], scalar=mod[:, 16 + c, 0:1], in1=xres[:, c, :],
                    op0=ALU.mult, op1=ALU.add).then_inc(S("wout_taken"), 1)
            apply_norm("norm2", xres, h2, TX, root, rstd, lambda c: coef2[:, c:c + 1], "h2_scaled")
            n = Tally(S("ffn_taps"))
            for j in range(2 * NG):
                dst = (g[:, j, :] if j < NG else acc[:, j % 2, :]).rearrange("p (r c) -> p r c", r=ROWS)
                src = bank(j % 4)[:, 0:TX].rearrange("p (r c) -> p r c", r=ROWS)
                dve.wait_ge(S("ffn_mid"), j + 1)
                for tap in range(9):
                    if tap == 4:
                        continue
                    dy, dx = tap // 3 - 1, tap % 3 - 1
                    r0, r1 = max(0, -dy), ROWS - max(0, dy)
                    c0, c1 = max(0, -dx), GRID - max(0, dx)
                    o = dst[:, r0:r1, c0:c1]
                    if tap > 0:
                        n.wait(dve)
                    n(stt(out=o, in0=src[:, r0 + dy:r1 + dy, c0 + dx:c1 + dx],
                          scalar=prm("ffn_conv", tap * 2 * NG + j), in1=o, op0=ALU.mult, op1=ALU.add))
            for c in range(KD):
                half, q = c // 4, c % 4
                if q < 3:
                    dve.wait_ge(S("down"), 3 * half + q + 1)
                else:
                    dve.wait_ge(S("down_read"), 3 * half + 3)
                stt(out=xres[:, c, :], in0=bank(4 * half + q)[:, 0:TX], scalar=mod[:, 40 + c, 0:1], in1=xres[:, c, :],
                    op0=ALU.mult, op1=ALU.add).then_inc(S("down_taken"), 1)
            apply_norm("final1", xres, H[:, :, META:L], TX, root, rstd, lambda c: prm("final_g", c), "H_ready")

            apply_norm("gmix", H, u, L, rt2, rs2, lambda c: prm("g_mix", c), "gmix_norm")
            n = Tally(S("lam_sums"))
            dve.wait_ge(S("lam_in"), 16)
            for q in range(2):
                n(V_.tensor_tensor_reduce(lam4[:, 2 * q, :], lam4[:, 2 * q, :], lam4[:, 2 * q + 1, :], 1.0, 0.0,
                                          ALU.mult, ALU.add, lam_s[:, q:q + 1]))
            ts(sub_gain, prm("subln"), 1.0 - LAM_INIT, None, ALU.mult).then_inc(S("sub_gain"), 1)
            for e in range(10):
                dve.wait_ge(S("V_turned"), e + 1)
                V_.tensor_copy(V[:, 0:2, e, :], bank(e % 4)[:, 0:2 * P].rearrange("p (t c) -> p t c", t=2))
                V_.tensor_copy(V[0:16, 2, e, :], bank(e % 4)[0:16, 2 * P:3 * P]).then_inc(S("V_kept"), 1)

            def qk(e):
                return qb[:, e, :] if e < 8 else kb[:, e - 8, :]

            def head_norm(name, head, count, gain):
                for e in range(count):
                    dve.wait_ge(S("head_roots"), HEAD_NORMS[name] + e + 1)
                    if e >= 1:
                        dve.wait_ge(S(name + "_normed"), e)
                    V_.reciprocal(rs2, rt2).then_inc(S("head_recips"), 1)
                    dve.wait_ge(S("head_recips"), HEAD_NORMS[name] + e + 1)
                    stt(out=head(e), in0=head(e), scalar=gain(e), in1=rs2, op0=ALU.mult, op1=ALU.mult)\
                        .then_inc(S(name + "_normed"), 1)

            head_norm("qk", qk, 10, lambda e: prm("qnorm") if e < 8 else prm("knorm"))
            for e in range(10):
                dve.wait_ge(S("qk_turned"), e + 1)
                if e >= 2:
                    dve.wait_ge(S("qk_rotated"), e - 1)
                dve.wait_ge(S("head_squares"), 10)
                tt(sqq[e % 2], bank(5 + e % 2)[:, 0:L], cst2("rope_sin"), ALU.mult).then_inc(S("qk_sined"), 1)
                tt(qk(e), qk(e), cst2("rope_cos"), ALU.mult).then_inc(S("qk_cosined"), 1)
                dve.wait_ge(S("qk_sined"), e + 1)
                dve.wait_ge(S("qk_cosined"), e + 1)
                tt(qk(e), qk(e), sqq[e % 2], ALU.add).then_inc(S("qk_rotated"), 1)
            n = Tally(S("lam_steps"))
            dve.wait_ge(S("lam_exp"), 1)
            n(ts(lam_s[:, 4:5], lam_s[:, 2:3], -1.0, -LAM_INIT, ALU.mult, ALU.add))
            n.wait(dve)
            n(tt(lam_s[:, 5:6], lam_s[:, 3:4], lam_s[:, 4:5], ALU.add))
            n.wait(dve)

            biased = Tally(S("biased"))
            maxed = Tally(S("maxed"))
            weighed = Tally(S("weigh_steps"))

            def maxima(n):
                un = units[n]
                nq = QC[un.tile][1]
                dve.wait_ge(S("scores"), n + 1)
                both = ps[0:nq, 2 * (n % 2):2 * (n % 2) + 2, 0:L]
                st = stat[n % 2]
                if n >= 2:
                    dve.wait_ge(S("scores_read"), n - 1)
                if un.diff:
                    slope = 2.0 ** (-8.0 * (un.head + 1) / AH)
                    dist = bc(cst2("dist%d" % un.tile)[0:nq, :].rearrange("p (o t) -> p o t", o=1), nq, 2, L)
                    biased(stt(out=sc[n % 2][0:nq, :, :], in0=dist, scalar=-slope * HEAD ** 0.5, in1=both,
                               op0=ALU.mult, op1=ALU.add))
                    biased.wait(dve)
                    both = sc[n % 2][0:nq, :, :]
                maxed(V_.tensor_reduce(st[0:nq, 0:2], both, AX, ALU.max))
                maxed.wait(dve)
                ts(st[0:nq, 2:4], st[0:nq, 0:2], -(HEAD ** -0.5 if un.diff else P ** -0.5), None, ALU.mult)\
                    .then_inc(S("maxima"), 1)

            def weights(n):
                un = units[n]
                nq = QC[un.tile][1]
                st, e = stat[n % 2], ee[n % 2]
                dve.wait_ge(S("scores_read"), n + 1)
                weighed(V_.reciprocal(st[0:nq, 6:8], st[0:nq, 4:6]))
                weighed.wait(dve)
                if un.diff:
                    weighed(tt(st[0:nq, 7:8], st[0:nq, 7:8], lam_s[0:nq, 5:6], ALU.mult))
                    weighed(ts(e[0:nq, 0, :], e[0:nq, 0, :], st[0:nq, 6:7], None, ALU.mult))
                    weighed.wait(dve)
                    stt(out=e[0:nq, 0, :], in0=e[0:nq, 1, :], scalar=st[0:nq, 7:8], in1=e[0:nq, 0, :], op0=ALU.mult,
                        op1=ALU.add).then_inc(S("weights"), 1)
                else:
                    for m in range(2):
                        ts(e[0:nq, m, :], e[0:nq, m, :], st[0:nq, 6 + m:7 + m], None, ALU.mult)\
                            .then_inc(S("weights"), 1)

            for n in range(len(units) + 1):
                if n < len(units):
                    maxima(n)
                if n >= 1:
                    weights(n - 1)
            dve.wait_ge(S("sub_gain"), 1)
            head_norm("oa", lambda e: oa[:, e, :], AH, lambda e: sub_gain)
            for j in range(KD):
                dve.wait_ge(S("branch_a"), j + 1)
                tt(ga[:, j, :], bank(j % 4)[:, 0:L], ga[:, j, :], ALU.mult).then_inc(S("branch_a_taken"), 1)
            n = Tally(S("branch_b_steps"))
            for j in range(KD):
                dve.wait_ge(S("branch_b"), j + 1)
                n(tt(gb[:, j, :], bank(j % 4)[:, 0:L], gb[:, j, :], ALU.mult))
                n.wait(dve)
                dve.wait_ge(S("branch_a_taken"), j + 1)
                n(tt(ga[:, j, :], ga[:, j, :], gb[:, j, :], ALU.add))
            for j in range(KD):
                dve.wait_ge(S("wout2"), j + 1)
                tt(H[:, j, :], bank(j % 4)[:, 0:L], H[:, j, :], ALU.add).then_inc(S("wout2_taken"), 1)
            apply_norm("gffn", H, u, L, rt2, rs2, lambda c: prm("g_ffn", c), "gffn_norm")

            n = Tally(S("router_steps"))
            parts = ((P, 0, 2), (16, 2, 3))
            dve.wait_ge(S("logits"), 1)
            for rows, t0, t1 in parts:
                n(V_.tensor_reduce(rstat[0:rows, t0:t1], bank(0)[0:rows, t0 * NE:t1 * NE]
                                   .rearrange("p (t e) -> p t e", e=NE), AX, ALU.max))
            n.wait(dve)
            for rows, t0, t1 in parts:
                tt(logit[0:rows, t0:t1, :], bank(0)[0:rows, t0 * NE:t1 * NE].rearrange("p (t e) -> p t e", e=NE),
                   bc(rstat[0:rows, t0:t1].rearrange("p (t o) -> p t o", o=1), rows, t1 - t0, NE), ALU.subtract)\
                    .then_inc(S("logits_shifted"), 1)
            dve.wait_ge(S("logits_exp"), 2)
            for rows, t0, t1 in parts:
                n(V_.tensor_reduce(rstat[0:rows, 3 + t0:3 + t1], aff[0:rows, t0:t1, :], AX, ALU.add))
            n.wait(dve)
            for rows, t0, t1 in parts:
                n(V_.reciprocal(rstat[0:rows, 3 + t0:3 + t1], rstat[0:rows, 3 + t0:3 + t1]))
            n.wait(dve)
            for rows, t0, t1 in parts:
                last = tt(aff[0:rows, t0:t1, :], aff[0:rows, t0:t1, :],
                          bc(rstat[0:rows, 3 + t0:3 + t1].rearrange("p (t o) -> p t o", o=1), rows, t1 - t0, NE),
                          ALU.mult)
            last.then_inc(S("aff"), 1)
            e16 = slice(0, NE)
            dve.wait_ge(S("aff_turned"), 1)
            n(V_.tensor_copy(aff_e[e16, :], bank(3)[e16, 0:L]))
            n.wait(dve)
            src = aff_e
            for _ in range((CAP - 1) // 8):
                n(V_.max(top8[e16, :], src[e16, :]))
                n.wait(dve)
                n(V_.match_replace(left[e16, :], top8[e16, :], src[e16, :], -1.0))
                n.wait(dve)
                src = left
            n(V_.max(top8[e16, :], left[e16, :]))
            n.wait(dve)
            last_in = top8[e16, (CAP - 1) % 8:(CAP - 1) % 8 + 1]
            n(ts(above[e16, :], aff_e[e16, :], last_in, None, ALU.is_gt))
            n(ts(equal[e16, :], aff_e[e16, :], last_in, None, ALU.is_equal))
            n.wait(dve)
            n(V_.tensor_reduce(counts[e16, 0:1], above[e16, :], AX, ALU.add))
            n(V_.tensor_tensor_scan(left[e16, :], equal[e16, :], equal[e16, :], 0.0, ALU.add, ALU.max))
            n.wait(dve)
            n(ts(counts[e16, 1:2], counts[e16, 0:1], -1.0, float(CAP), ALU.mult, ALU.add))
            n.wait(dve)
            n(stt(out=equal[e16, :], in0=left[e16, :], scalar=counts[e16, 1:2], in1=equal[e16, :], op0=ALU.is_le,
                  op1=ALU.mult))
            n.wait(dve)
            n(tt(above[e16, :], above[e16, :], equal[e16, :], ALU.add))
            n.wait(dve)
            n(V_.tensor_tensor_scan(left[e16, :], above[e16, :], above[e16, :], 0.0, ALU.add, ALU.max))
            n.wait(dve)
            tt(places[e16, :], left[e16, :], above[e16, :], ALU.mult).then_inc(S("places"), 1)
            dve.wait_ge(S("places_turned"), 1)
            for rows, t0, t1 in parts:
                n(V_.tensor_copy(placeT[0:rows, t0:t1, :], bank(4)[0:rows, t0 * NE:t1 * NE]
                                 .rearrange("p (t e) -> p t e", e=NE)))
            n.wait(dve)
            for t, (t0, nt) in enumerate(QC):
                slot = cst2("slot")[0:nt, :].rearrange("p (o s) -> p o s", o=1)
                n(tt(sel[0:nt, t, :, :], bc(placeT[0:nt, t, :].rearrange("p (e o) -> p e o", o=1), nt, NE, SLOTS),
                     bc(slot, nt, NE, SLOTS), ALU.is_equal))
            n.wait(dve)
            for t, (t0, nt) in enumerate(QC):
                last = tt(selA[0:nt, t, :, :], sel[0:nt, t, :, :],
                          bc(aff[0:nt, t, :].rearrange("p (e o) -> p e o", o=1), nt, NE, SLOTS), ALU.mult)
            last.then_inc(S("selA_ready"), 1)

            def pair(i):
                dve.wait_ge(S("silu"), i + 1)
                dve.wait_ge(S("up_e"), i + 1)
                tt(hid, bank(3), hgate, ALU.mult).then_inc(S("hid"), 1)
                for c in range(KD):
                    dve.wait_ge(S("spread"), i * KD + c + 1)
                    tt(H[:, c, :], bank(6 + c % 2)[:, 0:L], H[:, c, :], ALU.add).then_inc(S("added"), 1)
                dve.wait_ge(S("added"), i * KD + KD)

            with dve.Fori(0, NE // 2) as i:
                pair(i)
            apply_norm("last", H, H, L, rt2, rs2, lambda c: prm("g_final", c), "out_ready")

        @block.gpsimd
        def _(pool):
            G = nc.gpsimd
            tt = G.tensor_tensor
            for d in range(2):
                pool.wait_ge(S("sums"), d + 1)
                tt(cum_before[:, d, :, :], cum[:, d, :, :], cum_before[:, d, :, :], ALU.subtract)\
                    .then_inc(S("sums_before"), 1)
            pool.wait_ge(S("ka_rest"), 1)
            pool.wait_ge(S("kk_unit"), NJ)
            pool.wait_ge(S("proj"), 19)

            def steps(s, outputs):
                at = lambda d: 2 * s + d + 1
                n = Tally(S("keys_staged"), s * 14)
                for d in range(2):
                    t = token_at(s, d, outputs)
                    a = iclr[:, d, :, bass.ds(t, C)]
                    n(tt(T0[d], a, per_channel(prm("k_a", 0, NJ), NJ, C), ALU.mult))
                    n(tt(T1[d], a, kk[:, :, bass.ds(t, C)], ALU.mult))
                    n(G.tensor_copy(V0[d], v[:, :, bass.ds(t, C)]))
                    n.wait(pool)
                    n(tt(T0[d], T0[d], per_channel(ka_rest, NJ, C), ALU.add))
                    n.wait(pool)
                    n(tt(T0[d], T0[d], k[:, :, bass.ds(t, C)], ALU.mult))
                    n.wait(pool)
                    pool.wait_ge(S("decays"), at(d))
                    n(tt(KB[d][:, :, 0, :], T0[d], EI[d], ALU.mult))
                    n(tt(KB[d][:, :, 1, :], T1[d], EI[d], ALU.mult))
                n.wait(pool)
                pool.wait_ge(*turn("values_turned", s, 1))

            with pool.Fori(0, 4) as s:
                steps(s, False)
            with pool.Fori(4, 8) as s:
                steps(s, True)

            pool.wait_ge(S("state_kept"), 4 * 8)
            n = Tally(S("bonus_terms"))
            n(tt(t4, iclr[:, 0, :, TC:TB], iclr[:, 1, :, TC:TB], ALU.add))
            for other, op in ((per_channel(prm("k_a", 0, NJ), NJ, TX), ALU.mult),
                              (per_channel(ka_rest2, NJ, TX), ALU.add), (k[:, :, TC:TB], ALU.mult), (r, ALU.mult),
                              (per_channel(prm("r_k", 0, NJ), NJ, TX), ALU.mult)):
                n.wait(pool)
                n(tt(t4, t4, other, op))

            for j in range(NG):
                pool.wait_ge(S("ffn_act"), j + 1)
                pool.wait_ge(S("ffn_taps"), 8 * (NG + j + 1))
                tt(g[:, j, :], g[:, j, :], acc[:, (NG + j) % 2, :], ALU.mult).then_inc(S("ffn_mul"), 1)

            pool.wait_ge(*norm_root("final1"))
            pool.dma_start(H[:, :, 0:META], dram["meta"]).then_inc(S("meta_in"), 16)
            pool.dma_start(late, dram["consts2"]).then_inc(S("consts2_in"), 16)
            pool.dma_start(lam4.rearrange("p a b -> p (a b)"), dram["lambdas"].to_broadcast([P, 256]))\
                .then_inc(S("lam_in"), 16)
            pool.wait_ge(S("branch_a"), 1)
            pool.dma_start(router, dram["router"]).then_inc(S("router_in"), 16)


def blocks_of(w, rows, columns):
    k, n = w.shape
    out = []
    for n0 in range(0, n, columns):
        for k0 in range(0, k, rows * P):
            part = w[k0:k0 + rows * P, n0:n0 + columns]
            r, c = part.shape[0] // P, part.shape[1]
            b = np.zeros((P, WBLK), w.dtype)
            b[:, :r * c] = part.reshape(r, P, c).transpose(1, 0, 2).reshape(P, r * c)
            out.append(b)
    return out


def by_channel(v):
    t, c = v.shape
    return np.ascontiguousarray(v.T.reshape(c // P, P, t).transpose(1, 0, 2))


def laid_out(i):
    i = {k: np.asarray(v) for k, v in i.items()}
    f = np.float32
    vec = lambda v: np.asarray(v).reshape(-1, P).T
    params = {
        "ada_b": i["ada_b"][0], "norm1_g": i["norm1_g"][0], "norm2_g": i["norm2_g"][0], "conv": i["rwkv_conv_w"][0],
        "w0": i["decay_w0"][0], "a0": i["iclr_a0"][0], "k_k": i["k_k"][0], "k_a": i["k_a"][0], "r_k": i["r_k"][0],
        "gn_g": i["gn_g"][0], "gn_b": i["gn_b"][0], "fourier_g": i["fourier_g"][0], "ffn_conv": i["ffn_conv_w"][0],
        "ffn_b": i["ffn_conv_b"][0], "final_g": i["final_g"], "g_mix": i["g_mix_2"][0], "subln": i["g_subln_2"][0],
        "qnorm": i["g_qnorm_2"][0], "knorm": i["g_knorm_2"][0], "g_ffn": i["g_ffn_2"][0], "g_final": i["g_final_2"]}
    blocks = (blocks_of(i["ada_w"][0], 8, 512) + blocks_of(i["w_in"][0], 8, 512) + blocks_of(i["w_out"][0], 8, 512)
              + blocks_of(i["ffn_w_up"][0], 8, 512) + blocks_of(i["ffn_w_down"][0], 8, 512)
              + blocks_of(i["w_in_2"][0], 8, 512) + blocks_of(i["w_branch_a_2"][0], 8, 512)
              + blocks_of(i["w_branch_b_2"][0], 8, 512) + blocks_of(i["w_out_2"][0], 8, 512))
    experts = []
    for e in range(0, NE, 2):
        experts += [blocks_of(i[n][0, e + k], r, c)[0] for n, r, c in
                    (("w_gate_2", 8, 512), ("w_up_2", 8, 512), ("w_down_2", 4, 1024)) for k in range(2)]
    table = constant_tables()
    return {
        "consts": np.ascontiguousarray(np.concatenate([table[n] for n in CONST], axis=1).astype(f)),
        "consts2": np.ascontiguousarray(np.concatenate([table[n] for n in CONST2], axis=1).astype(f)),
        "params": np.ascontiguousarray(np.concatenate([vec(params[n]) for n in PARAM], axis=1)),
        "cond": np.ascontiguousarray(np.stack([vec(i["c"][0]), vec(i["c_ctx"])], axis=2)),
        "tokens": np.concatenate([by_channel(i["ctx"][0]), by_channel(i["x"][0])], axis=2),
        "meta": by_channel(i["meta_tokens_2"]),
        "weights": np.stack(blocks),
        "experts": np.stack(experts),
        "decay_w2": np.ascontiguousarray(i["decay_w2"][0].reshape(P, RW)),
        "iclr_a2": np.ascontiguousarray(i["iclr_a2"][0].reshape(P, RW)),
        "gate_g2": np.ascontiguousarray(i["gate_g2"][0]),
        "router": np.ascontiguousarray(i["w_router_2"][0].reshape(KD, P, NE).transpose(1, 0, 2)),
        "lambdas": np.concatenate([i[n] for n in ("lambda_q1_2", "lambda_k1_2", "lambda_q2_2", "lambda_k2_2")],
                                  axis=1),
    }


def kernel(**inputs):
    import concourse.bacc as bacc
    from concourse.bass_utils import run_bass_kernel_spmd

    nc = bacc.Bacc("TRN2", target_bir_lowering=False, num_devices=1)
    arrays = laid_out(inputs)
    dram = {k: nc.dram_tensor(k, v.shape, mybir.dt.from_np(v.dtype), kind="ExternalInput").ap()
            for k, v in arrays.items()}
    out = nc.dram_tensor("out", (P, KD, TX), F32, kind="ExternalOutput").ap()
    two_blocks(nc, dram, out)
    r = run_bass_kernel_spmd(nc, [arrays], core_ids=[0])
    got = r.results[0]["out"]
    return np.ascontiguousarray(got.transpose(2, 1, 0).reshape(1, TX, D))
```

```python
from contextlib import ExitStack
import math

import numpy as np

import concourse.bass as bass
from concourse import mybir

ALU = mybir.AluOpType
ACT = mybir.ActivationFunctionType
AX = mybir.AxisListType.X
F32 = mybir.dt.float32
P = 128

D = 1024
KD = D // P
TX = 256
TC = 256
TB = TX + TC
FW = 512
RW = 512
HEAD = 64
NJ = RW // P
C = 64
DFF = 2816
NG = DFF // P
GRID = 64
ROWS = TX // GRID
EPS = 1e-6
GN_EPS = 64e-5
KK_EPS = 1e-12
LOG_DECAY = math.exp(-0.5)

META = 16
L = META + TX
QC = ((0, 128), (128, 128), (256, 16))
AH = 8
BH = 8
QK_NORM = 37
NE = 16
EFF = 512
CAP = 2 * L // NE
SLOTS = 64
LAM_INIT = 0.8 - 0.6

W_ADA, W_IN, W_OUT, W_UP, W_DOWN, W_IN2, W_B, W_A, W_OUT2, W_END = 0, 4, 9, 11, 22, 28, 41, 43, 45, 47
ZEROED = 6
PIECE = 256
RING = 4
WBLK = 4096


def block_columns(b):
    return 384 if b == W_OUT - 1 else 512


def block_rows(b):
    return 6 if b in (W_DOWN + 2, W_DOWN + 5) else 8


def constant_tables():
    t = {}
    i = np.arange(P)
    t["ident"] = np.eye(P)
    t["ones"] = np.ones((P, P))
    t["headones"] = (i[:, None] // 64 == i[None, :] // 64).astype(float)
    t["sign"] = np.where(i < 64, 1.0, -1.0)[:, None]
    a, b = i[:, None], i[None, :]
    same_head = a // 64 == b // 64
    same_8 = a // 8 == b // 8
    for d in range(2):
        before = (a < b) if d == 0 else (a > b)
        after = (a > b) if d == 0 else (a < b)
        t[f"diagT{d}"] = -1.0 * (same_head & same_8 & before)
        t[f"offT{d}"] = -1.0 * (same_head & ~same_8 & before)
        t[f"diag{d}"] = -1.0 * (same_head & same_8 & after)
        wide = np.arange(2 * P)[None, :]
        ra, cb = a % 64, wide % 64
        strict = (ra < cb) if d == 0 else (ra > cb)
        incl = strict | (ra == cb)
        t[f"gram{d}"] = np.where(wide < P, strict & (a < 64), incl) * np.where(a < 64, 1.0, -1.0)
        tok = np.arange(TB) % C
        t[f"keep{d}"] = np.tile((tok != (0 if d == 0 else C - 1)).astype(float), (P, 1))
    g = FW // 8
    cc = np.arange(g)
    ang = 2 * np.pi * np.outer(cc, cc) / g
    for name, f in (("chan_cos", np.cos), ("chan_sin", np.sin)):
        m = np.zeros((P, P))
        m[:64, :64] = m[64:, 64:] = f(ang)
        t[name] = m
    tt = np.arange(TX)
    ang = 2 * np.pi * (np.outer(tt, tt) % TX) / TX
    scale = 1.0 / math.sqrt(TX * g)
    for k in range(2):
        t[f"tok_cos{k}"] = np.cos(ang)[k * P:(k + 1) * P] * scale
        t[f"tok_sin{k}"] = -np.sin(ang)[k * P:(k + 1) * P] * scale
    rot = np.zeros((P, P))
    half, quarter = 64, 32
    for base in (0, half):
        for m in range(quarter):
            rot[base + quarter + m, base + m] = -1.0
            rot[base + m, base + quarter + m] = 1.0
    t["rotate"] = rot
    inv = (np.float32(10000.0) ** (-np.arange(0, half, 2, dtype=np.float32) / np.float32(half))).astype(np.float32)
    n = np.arange(TX)
    row = np.concatenate([np.zeros(META), n // GRID]).astype(np.float32)
    col = np.concatenate([np.zeros(META), n % GRID]).astype(np.float32)
    ang = np.concatenate([np.tile((inv[:, None] * row[None, :]), (2, 1)),
                          np.tile((inv[:, None] * col[None, :]), (2, 1))]).astype(np.float32)
    t["rope_cos"] = np.cos(ang)
    t["rope_sin"] = np.sin(ang)
    pos = np.arange(L)
    dist = np.abs(pos[:, None] - pos[None, :]).astype(float)
    dist[:META, :] = 0
    dist[:, :META] = 0
    for k, (q0, nq) in enumerate(QC):
        m = np.zeros((P, L))
        m[:nq] = dist[q0:q0 + nq]
        t[f"dist{k}"] = m
    t["slot"] = np.tile(np.arange(1, SLOTS + 1, dtype=float), (P, 1))
    return t


def placed(names_and_widths):
    at, out = 0, {}
    for n, w in names_and_widths:
        out[n] = (at, w)
        at += w
    return out, at


LATE = ("rotate", "rope_cos", "rope_sin", "dist0", "dist1", "dist2", "slot")
_widths = [(n, v.shape[1]) for n, v in constant_tables().items()]
CONST, NCONST = placed([x for x in _widths if x[0] not in LATE])
CONST2, NCONST2 = placed([x for x in _widths if x[0] in LATE])

PARAM_SIZES = [("ada_b", 48), ("norm1_g", 8), ("norm2_g", 8), ("conv", 36), ("w0", 8), ("a0", 8), ("k_k", 4),
               ("k_a", 4), ("r_k", 4), ("gn_g", 4), ("gn_b", 4), ("fourier_g", 4), ("ffn_conv", 9 * 44),
               ("ffn_b", 44), ("final_g", 8), ("g_mix", 8), ("subln", 1), ("qnorm", 1), ("knorm", 1),
               ("g_ffn", 8), ("g_final", 8)]
PARAM = {}
_at = 0
for _n, _c in PARAM_SIZES:
    PARAM[_n] = _at
    _at += _c
NPARAM = _at


class Places:

    def __init__(self, tensor, start, end):
        self.tensor, self.at, self.end = tensor, start, end

    def take(self, *shape):
        n = int(np.prod(shape))
        v = self.tensor[:, self.at:self.at + n]
        self.at += n
        assert self.at <= self.end, (self.at, self.end)
        if len(shape) == 2:
            return v.rearrange("p (a b) -> p a b", a=shape[0])
        if len(shape) == 3:
            return v.rearrange("p (a b c) -> p a b c", a=shape[0], b=shape[1])
        if len(shape) == 4:
            return v.rearrange("p (a b c d) -> p a b c d", a=shape[0], b=shape[1], c=shape[2])
        return v


class Tally:

    def __init__(self, sem, start=0):
        self.sem, self.n = sem, start

    def __call__(self, instruction):
        instruction.then_inc(self.sem, 1)
        self.n = self.n + 1

    def wait(self, engine):
        engine.wait_ge(self.sem, self.n)


class Unit:

    def __init__(self, diff, head, tile, first_map, out_head):
        self.diff, self.head, self.tile = diff, head, tile
        self.maps = 1 if diff else 2
        self.first_map, self.out_head = first_map, out_head


def attention_units():
    out = [Unit(True, hd, t, 3 * hd + t, hd) for hd in range(AH) for t in range(3)]
    n = len(out)
    for hd in range(0, BH, 2):
        for t in range(3):
            out.append(Unit(False, hd, t, n, AH + hd))
            n += 2
    return out


def two_blocks(nc, dram, out):
    with ExitStack() as ctx:
        mem = ctx.enter_context(nc.sbuf_tensor("mem", [P, (nc.sbuf_usable_end - nc.sbuf_base) // 64 * 16 - 16], F32))
        ps = ctx.enter_context(nc.psum_tensor("ps", [P, 8, 512], F32))
        sems = {}

        def S(name):
            if name not in sems:
                sems[name] = ctx.enter_context(nc.semaphore(name))
            return sems[name]

        def bank(b):
            return ps[:, b, :]

        total = mem.shape[1]
        whole = Places(mem, 0, total)
        ring_at = whole.at
        ring = [whole.take(WBLK) for _ in range(RING)]
        consts = whole.take(NCONST)
        params = whole.take(NPARAM)
        mod = whole.take(48, 2)
        coef1 = whole.take(KD, 2)
        coef2 = whole.take(KD)
        cond = whole.take(KD, 2)
        cond_act = whole.take(KD, 2)
        ka_rest = whole.take(NJ)
        ka_rest2 = whole.take(NJ)
        tokens = whole.take(KD, TB)
        xres = tokens[:, :, TC:TB]
        arena = whole.at

        def cst(name):
            a, n = CONST[name]
            return consts[:, a:a + n]

        def prm(name, i=0, n=1):
            return params[:, PARAM[name] + i:PARAM[name] + i + n]

        ident = cst("ident")

        m1 = Places(mem, arena, total)
        h = m1.take(KD, TB)
        squares = m1.take(KD, TB)
        r = m1.take(NJ, TX)
        k = m1.take(NJ, TB)
        v = m1.take(NJ, TB)
        kk = m1.take(NJ, TB)
        four = m1.take(NJ, TX)
        cum = m1.take(2, NJ, TB)
        wd = m1.take(TB)
        ad = m1.take(TB)
        gd = m1.take(TX)
        y = m1.take(2, NJ, TX)
        root = m1.take(TB)
        rstd = m1.take(TB)
        gate_w = m1.take(RW)
        late_ada = m1.take(KD, PIECE)
        at_h = Places(mem, arena, total)
        cum_before = at_h.take(2, NJ, TB)
        iclr = at_h.take(2, NJ, TB)
        at_cum = Places(mem, 16384 + arena, total)
        assert at_cum.at == arena + 2 * KD * TB + NJ * TX + 3 * NJ * TB + NJ * TX
        spectrum = at_cum.take(2, NJ, 2 * P)
        mod_rows = at_cum.take(2, 512)
        y_at = at_cum.at + 512 + 512 + 256
        at_y = Places(mem, y_at + 1024, total)
        decay_w = at_y.take(2, RW)
        iclr_w = at_y.take(2, RW)
        kk_sq = at_cum.take(2, TB)

        kk_root = late_ada.rearrange("p k c -> p (k c)").rearrange("p (j t) -> p j t", j=NJ)

        ms = Places(mem, ring_at, ring_at + RING * WBLK)
        KB = [ms.take(NJ, 2, C) for _ in range(2)]
        KR = [ms.take(NJ, 2, 2, C) for _ in range(2)]
        RB = [ms.take(NJ, 2, C) for _ in range(2)]
        EC = [ms.take(NJ, C) for _ in range(2)]
        EP = [ms.take(NJ, C) for _ in range(2)]
        EI = [ms.take(NJ, C) for _ in range(2)]
        GM = [ms.take(NJ, 2, 2, C) for _ in range(2)]
        VU = [ms.take(NJ, P) for _ in range(2)]
        KBT = [ms.take(NJ, P) for _ in range(2)]
        Q = [ms.take(NJ, P) for _ in range(2)]
        B1, B2, B3, B4, B5 = ([ms.take(NJ, P) for _ in range(2)] for _ in range(5))
        late_rows = ms.take(2, PIECE)
        spare = [tokens[:, i, 0:TC].rearrange("p (j c) -> p j c", j=NJ) for i in range(KD)]
        V0, X, T0, T1 = spare[0:2], spare[2:4], spare[4:6], spare[6:8]

        ST = [x.rearrange("p (j c) -> p j c", j=NJ) for x in (root, rstd)]
        EW = [x.rearrange("p (j c) -> p j c", j=NJ) for x in (wd, ad)]

        mp = Places(mem, arena + 16384, total)
        rw = mp.take(NJ, TX)
        bonus = mp.take(NJ, TX)
        ysq = mp.take(NJ, TX)
        t4 = mp.take(NJ, TX)
        mf = Places(mem, arena, total)
        h2 = mf.take(KD, TX)
        sq2 = mf.take(KD, TX)
        g = mf.take(NG, TX)
        acc = mf.take(2, TX)

        squares_f = spectrum.rearrange("p a b c -> p (a b c)")[:, 0:NJ * TX].rearrange("p (k t) -> p k t", k=NJ)

        m2 = Places(mem, arena, total)
        H = m2.take(KD, L)
        u = m2.take(KD, L)
        late = m2.take(NCONST2)
        lam_s = m2.take(8)
        sub_gain = m2.take(1)
        rt2 = m2.take(L)
        rs2 = m2.take(L)
        sqq = [m2.take(L) for _ in range(2)]
        lam4 = Places(mem, m2.at - 2 * L, total).take(4, 64)
        expert_at = m2.at
        qa = m2.take(AH, L)
        ka = m2.take(AH, L)
        va = m2.take(AH, L)
        qb = m2.take(BH, L)
        kb = m2.take(2, L)
        vb = m2.take(2, L)
        ga = m2.take(KD, L)
        gb = m2.take(KD, L)
        V = m2.take(3, 10, P)
        oa, ob = va, ka
        sined = [V[:, 0, 4 * i:4 * i + 3, :].rearrange("p a b -> p (a b)")[:, 0:L] for i in range(2)]
        sqV = V.rearrange("p a b c -> p (a b c)")[:, 0:KD * L].rearrange("p (k t) -> p k t", k=KD)
        mx = Places(mem, arena - KD * TB, arena)
        sc = [mx.take(2, L) for _ in range(2)]
        ee = [mx.take(2, L) for _ in range(2)] + [Places(mem, arena + KD * L, total).take(2, L)]
        WT = [mx.take(3, L) for _ in range(2)]
        stat = [mx.take(8) for _ in range(3)]
        units = attention_units()

        def cst2(name):
            a, n = CONST2[name]
            return late[:, a:a + n]

        me = Places(mem, expert_at, total)
        utok = me.take(3, D)
        sel = me.take(3, NE, SLOTS)
        xring = [me.take(WBLK) for _ in range(2)]
        selT = me.take(NE // 2, L)
        xsT = me.take(KD, P)
        hid = me.take(EFF)
        hidT = me.take(EFF // P, P)
        yexp = me.take(D)
        eslots = ring + xring
        sqq8 = utok.rearrange("p t d -> p (t d)")[:, 0:KD * L].rearrange("p (k t) -> p k t", k=KD)
        mt = Places(mem, expert_at + 3 * D + 3 * NE * SLOTS + 2 * WBLK, total)
        aff_e, left, above, equal, places = (mt.take(L) for _ in range(5))
        sg = Places(mem, arena - KD * TB, arena)
        selA = sg.take(3, NE, SLOTS)
        router = sg.take(KD, NE)
        hgate = sg.take(EFF)
        logit = sg.take(3, NE)
        aff = sg.take(3, NE)
        placeT = sg.take(3, NE)
        rstat = sg.take(8)
        top8 = sg.take(8)
        counts = sg.take(2)

        last_use = {}
        for n in range(W_IN):
            last_use[n] = ("mod_rows", n + 1)
        dense = {"proj": (W_IN, W_OUT), "wout": (W_OUT, W_UP), "up": (W_UP, W_DOWN), "proj2": (W_IN2, W_B),
                 "branch_b": (W_B, W_A), "branch_a": (W_A, W_OUT2), "wout2": (W_OUT2, W_END)}
        for name, (b0, b1) in dense.items():
            n = 0
            for b in range(b0, b1):
                n += block_columns(b) // P
                last_use[b] = (name, n)
        for n in range(6):
            last_use[W_DOWN + n] = ("down_read", n + 1)
        use = {b: S("ring%d" % (b % RING)) for b in range(RING)}

        def load_block(sp, b, free=True):
            if b >= RING and free:
                sp.wait_ge(S(last_use[b - RING][0]), last_use[b - RING][1])
            n = block_rows(b) * block_columns(b)
            sp.dma_start(ring[b % RING][:, 0:n], dram["weights"][b, :, 0:n]).then_inc(use[b % RING], 16)

        def have_block(engine, b):
            engine.wait_ge(use[b % RING], 16 * (b // RING + 1))

        def block_view(b):
            n = block_rows(b) * block_columns(b)
            return ring[b % RING][:, 0:n].rearrange("p (k c) -> p k c", k=block_rows(b))

        block = ctx.enter_context(nc.Block())

        NORMS = {"norm1": (0, 0), "four": (1, 8), "norm2": (2, 12), "final1": (3, 20), "gmix": (4, 28),
                 "gffn": (5, 36), "last": (6, 44)}
        HEAD_NORMS = {"qk": 0, "oa": 10}

        def norm_root(name):
            return S("norm_roots"), NORMS[name][0] + 1

        JOBS = {"tiles_made": ("gram0", "gram1", "removalsT", "removals", "keys_turned", "values_turned", "A2",
                               "A2T", "A4", "Q1", "Q2", "inverse8", "M",
                               "MT", "M2", "M2T", "R1", "M4", "R2",
                               "held", "R3", "removed", "state_made"),
                "kept_by_scalar": ("keys_kept", "values_kept", "A2_kept", "A2T_kept", "A4_kept", "inverse8_kept",
                               "M_kept", "MT_kept", "M2_kept", "M2T_kept", "M4_kept", "held_kept",
                               "removed_kept"),
                "kept_by_vector": ("gram0_kept", "gram1_kept", "A_kept", "Q0_kept", "Q1_kept", "Q2_kept",
                               "R1_kept", "R2_kept", "R3_kept")}

        def turns_of(name):
            return S([k for k, jobs in JOBS.items() if name in jobs][0])

        def turn(name, s, d):
            jobs = [jobs for jobs in JOBS.values() if name in jobs][0]
            return turns_of(name), s * (2 * len(jobs)) + (2 * jobs.index(name) + d + 1)

        def free_bank(engine, name, n, banks=4):
            if n >= banks:
                engine.wait_ge(S(name + "_taken"), n - banks + 1)

        def proj_taken(engine, j):
            if j < 4:
                engine.wait_ge(S("proj_taken"), j + 1)
            elif j < 16:
                engine.wait_ge(S("conv_steps"), 2 * (j - 3))
            else:
                engine.wait_ge(S("proj_taken"), j - 11)

        @block.sync
        def _(sp):
            sp.dma_start(cond, dram["cond"]).then_inc(S("cond_in"), 16)
            load_block(sp, 0)
            sp.dma_start(tokens, dram["tokens"]).then_inc(S("tokens_in"), 16)
            sp.dma_start(consts, dram["consts"]).then_inc(S("consts_in"), 16)
            for b in range(1, W_OUT):
                load_block(sp, b)
            sp.wait_ge(S("kk_recip"), NJ)
            with sp.Fori(0, 8) as s:
                for piece in range(2):
                    sp.wait_ge(S("mod_rows"), 2 * s + (W_IN + piece))
                    sp.dma_start(late_ada.rearrange("p k c -> p (k c)"),
                                 dram["late_ada"][bass.ds(2 * s + piece, 1), :, :].rearrange("o p n -> (o p) n"))\
                        .then_inc(S("late_ada_in"), 16)
            sp.wait_ge(S("state_kept"), ZEROED + 4 * 8)
            sp.wait_ge(S("y_kept"), 2 * 4)
            for b in range(W_OUT, W_END):
                load_block(sp, b, free=b >= W_OUT + RING)
            for s in range(6):
                if s < 4:
                    b = W_END - RING + (s - W_END % RING) % RING
                    sp.wait_ge(S(last_use[b][0]), last_use[b][1])
                else:
                    sp.wait_ge(S("gffn_norm"), KD)
                sp.dma_start(eslots[s], dram["experts"][s, :, :]).then_inc(S("eslot%d" % s), 16)
            with sp.Fori(1, NE // 2) as i:
                for s in range(6):
                    sp.wait_ge(S(("gate", "up_e", "down_e")[s // 2]), i * (2 if s >= 4 else 1))
                    sp.dma_start(eslots[s], dram["experts"][bass.ds(i * 6 + s, 1), :, :]
                                 .rearrange("o p n -> (o p) n")).then_inc(S("eslot%d" % s), 16)
            sp.wait_ge(S("out_ready"), KD)
            sp.dma_start(out, H[:, :, META:L]).then_inc(S("out_written"), 16)
            sp.wait_ge(S("out_written"), 16)

        @block.tensor
        def _(pe):
            mm = nc.tensor.matmul

            def norm_sums(name, sq, chunks, n, b):
                for c in range(chunks):
                    pe.wait_ge(S("norm_squares"), NORMS[name][1] + c + 1)
                    last = mm(bank(b)[:, 0:n], cst("ones"), sq[:, c, 0:n], start=c == 0, stop=c == chunks - 1)
                last.then_inc(S("norm_sums"), 1)

            def dense_product(name, rhs, n, wait_rhs=None, banks=4, width=None, wait_bank=None, after=None):
                b0, b1 = dense[name]
                j = 0
                for b in range(b0, b1):
                    have_block(pe, b)
                    w = block_view(b)
                    for c in range(block_columns(b) // P):
                        if wait_bank:
                            if j >= banks:
                                wait_bank(pe, j - banks)
                        else:
                            free_bank(pe, name, j, banks)
                        nn, rr = width(j) if width else (n, rhs)
                        for kc in range(KD):
                            if j == 0 and wait_rhs:
                                wait_rhs(kc)
                            last = mm(bank(j % banks)[:, 0:nn], w[:, kc, c * P:(c + 1) * P], rr(kc),
                                      start=kc == 0, stop=kc == KD - 1)
                        last.then_inc(S(name), 1)
                        if after:
                            after(j)
                        j += 1

            def turn_mod(n):
                pe.wait_ge(S("mod_rows_kept"), n + 1)
                for c in range(4):
                    i = 4 * n + c
                    last = nc.tensor.transpose(bank(2)[:, 2 * i:2 * i + 2], mod_rows[0:2, n % 2, c * P:(c + 1) * P],
                                               ident[0:2, 0:2])
                last.then_inc(S("mod_turned"), 1)

            pe.wait_ge(S("cond_act"), 1)
            for n in range(W_IN):
                have_block(pe, n)
                if n >= 2:
                    pe.wait_ge(S("mod_rows_kept"), n - 1)
                for kc in range(KD):
                    last = mm(bank(n % 2)[0:2, :], cond_act[:, kc, :], block_view(n)[:, kc, :],
                              start=kc == 0, stop=kc == KD - 1)
                last.then_inc(S("mod_rows"), 1)
                if n == 0:
                    pe.wait_ge(S("consts_in"), 16)
                    norm_sums("norm1", squares, KD, TB, 7)
                if n >= 1:
                    turn_mod(n - 1)
            turn_mod(W_IN - 1)

            pe.wait_ge(S("mod_kept"), 1)
            dense_product("proj", None, None,
                          wait_rhs=lambda kc: pe.wait_ge(S("h_ready"), 2 * (kc + 1)),
                          width=lambda j: ((TX, lambda kc: h[:, kc, TC:TB]) if j < 8 or j == 18
                                           else (TB, lambda kc: h[:, kc, :])),
                          wait_bank=proj_taken)

            pe.wait_ge(*norm_root("norm1"))
            for j in range(NJ):
                pe.wait_ge(S("kk_squares"), j + 1)
                mm(bank(4 + j), cst("headones"), kk_sq[:, j % 2, :], start=True, stop=True).then_inc(S("kk_sums"), 1)

            pe.wait_ge(S("lora_in"), 32)
            pe.wait_ge(S("kk_root"), 2)
            pe.wait_ge(S("proj_taken"), 7)
            n = 0
            for w, src in ((decay_w, wd), (iclr_w, ad)):
                for d in range(2):
                    for j in range(NJ):
                        if n >= 2:
                            pe.wait_ge(S("lora_taken"), n - 1)
                        mm(bank(4 + n % 2), w[:, d, j * P:(j + 1) * P], src,
                           start=True, stop=True).then_inc(S("lora"), 1)
                        n += 1

            pe.wait_ge(S("kk_root"), NJ)
            for t in range(2):
                for jj in range(2):
                    n = 2 * t + jj
                    if n >= 2:
                        pe.wait_ge(S("spectrum_kept"), n - 1)
                    for q in range(2):
                        j = 2 * jj + q
                        last = mm(bank(6 + n % 2)[:, q * 256:q * 256 + 256], four[:, j, t * P:(t + 1) * P],
                                  consts[:, CONST["chan_cos"][0]:CONST["chan_cos"][0] + 2 * P],
                                  start=True, stop=True)
                    last.then_inc(S("spectrum"), 1)
            for jj in range(2):
                pe.wait_ge(S("spectrum_kept"), 4)
                for q in range(2):
                    j = 2 * jj + q
                    i = 0
                    for t in range(2):
                        for part, table in ((0, "tok_cos%d"), (1, "tok_sin%d")):
                            last = mm(bank(6 + jj)[:, q * 256:q * 256 + 256], spectrum[:, t, j, part * P:(part + 1) * P],
                                      cst(table % t), start=i == 0, stop=i == 3)
                            i += 1
                last.then_inc(S("mixed"), 1)

            pe.wait_ge(S("mixed_kept"), 2)
            norm_sums("four", squares_f, NJ, TX, 6)
            pe.wait_ge(*norm_root("four"))
            pe.wait_ge(S("lora_taken"), 16)
            pe.wait_ge(S("state_kept"), ZEROED)

            def B(d, i):
                return bank(4 * d + i)

            def late_piece(s, piece):
                pe.wait_ge(S("late_ada_in"), 32 * s + 16 * (piece + 1))
                pe.wait_ge(S("mod_rows_kept"), 2 * s + (W_IN + piece))
                for kc in range(KD):
                    last = mm(bank(7)[0:2, 256:256 + PIECE], cond_act[:, kc, :], late_ada[:, kc, :],
                              start=kc == 0, stop=kc == KD - 1)
                last.then_inc(S("mod_rows"), 1)

            def turn_piece(s, piece):
                for c in range(2):
                    at = 256 + 4 * piece + 2 * c
                    last = nc.tensor.transpose(bank(3)[:, at:at + 2], late_rows[0:2, piece, c * P:(c + 1) * P],
                                               ident[0:2, 0:2])
                last.then_inc(S("mod_turned"), 1)

            def steps(s, outputs):
                at = lambda d: 2 * s + d + 1
                cols = 2 * P if outputs else P
                flat = lambda x: x.rearrange("p h c -> p (h c)")

                def tiles(name, b, one, *waits):
                    for d in range(2):
                        for w in waits:
                            pe.wait_ge(*turn(w, s, d))
                        for j in range(NJ):
                            last = one(d, j, B(d, b)[:, j * P:(j + 1) * P])
                        last.then_inc(turns_of(name), 1)

                def product(lhs, rhs):
                    return lambda d, j, o: mm(o, lhs[d][:, j, :], rhs[d][:, j, :], start=True, stop=True)

                late_piece(s, 0)
                pe.wait_ge(S("mod_kept"), s + 1)
                pe.wait_ge(S("state_kept"), 4 * s + ZEROED)
                for q in range(2):
                    for d in range(2):
                        if q == 0:
                            pe.wait_ge(S("keys_staged"), s * 16 + 8 * (d + 1))
                            pe.wait_ge(S("reads_staged"), 2 * at(d))
                            if outputs:
                                pe.wait_ge(S("outs_staged"), 2 * at(d) - 16)
                        for j in (2 * q, 2 * q + 1):
                            last = mm(B(d, q)[:, (j % 2) * 2 * P:(j % 2) * 2 * P + cols], flat(KB[d][:, j, :, :]),
                                      KR[d][:, j, :, :, :].rearrange("p a h c -> p (a h c)")[:, 0:cols],
                                      start=True, stop=True)
                        last.then_inc(turns_of("gram%d" % q), 1)
                tiles("removalsT", 2, lambda d, j, o: mm(o, flat(RB[d][:, j, :, :]), flat(KR[d][:, j, 0, :, :]),
                                                         start=True, stop=True))
                pe.wait_ge(S("mod_rows_kept"), 2 * s + (W_IN + 1))
                tiles("removals", 3, lambda d, j, o: mm(o, flat(KR[d][:, j, 0, :, :]), flat(RB[d][:, j, :, :]),
                                                        start=True, stop=True))
                tiles("keys_turned", 0, lambda d, j, o: nc.tensor.transpose(o, flat(KB[d][:, j, :, :]), ident),
                      "gram0_kept", "gram1_kept")
                tiles("values_turned", 1, lambda d, j, o: nc.tensor.transpose(o[0:64, :], V0[d][:, j, :], ident))

                tiles("A2", 2, product(B1, B2), "A_kept")
                tiles("A2T", 3, product(B2, B1))
                tiles("A4", 0, product(B4, B3), "A2_kept", "A2T_kept", "keys_kept")
                tiles("Q1", 1, product(B3, Q), "values_kept", "Q0_kept")
                tiles("Q2", 2, product(B1, Q), "A4_kept", "Q1_kept")
                tiles("inverse8", 3, lambda d, j, o: nc.tensor.transpose(o, Q[d][:, j, :], ident), "Q2_kept")
                tiles("M", 0, product(B5, B2), "inverse8_kept")
                tiles("MT", 1, product(B2, B5))
                tiles("M2", 2, product(B4, B3), "M_kept", "MT_kept")
                tiles("M2T", 3, product(B3, B4))
                tiles("R1", 0, product(B3, Q))
                tiles("M4", 1, product(B5, B1), "M2_kept", "M2T_kept")
                tiles("R2", 2, product(B1, Q), "R1_kept")
                for d in range(2):
                    for j in range(NJ):
                        for p in range(2):
                            o = B(d, 3)[64 * p:64 * p + 64, j * C:(j + 1) * C]
                            mm(o, KR[d][:, j, 0, p, :], ST[d][:, j, p * C:(p + 1) * C], start=True, stop=False)
                            last = mm(o, GM[d][:, j, 0, p, :], VU[d][:, j, p * C:(p + 1) * C], start=False, stop=True)
                    last.then_inc(turns_of("held"), 1)
                tiles("R3", 0, product(B2, Q), "M4_kept", "R2_kept", "held_kept")
                turn_piece(s, 0)
                late_piece(s, 1)
                for d in range(2):
                    pe.wait_ge(*turn("R3_kept", s, d))
                    pe.wait_ge(*turn("held_kept", s, d))
                    for j in range(NJ):
                        for p in range(2):
                            last = mm(B(d, 1 + p)[64:128, j * C:(j + 1) * C], Q[d][:, j, p * C:(p + 1) * C],
                                      X[d][:, j, :], start=True, stop=True)
                    last.then_inc(turns_of("removed"), 1)
                pe.wait_ge(S("mod_rows_kept"), 2 * s + (W_IN + 2))
                for d in range(2):
                    pe.wait_ge(*turn("removed_kept", s, d))
                    for j in range(NJ):
                        last = mm(B(d, 0)[:, j * P:(j + 1) * P], KBT[d][:, j, :], VU[d][:, j, :], start=True, stop=True)
                    last.then_inc(turns_of("state_made"), 1)
                    if d == 0:
                        turn_piece(s, 1)
                    if outputs:
                        for j in range(NJ):
                            for p in range(2):
                                o = B(d, 3)[64 * p:64 * p + 64, j * C:(j + 1) * C]
                                mm(o, VU[d][:, j, p * C:(p + 1) * C], GM[d][:, j, 1, p, :], start=True, stop=False)
                                last = mm(o, ST[d][:, j, p * C:(p + 1) * C], KR[d][:, j, 1, p, :], start=False, stop=True)
                        last.then_inc(S("y_made"), 1)
                if outputs:
                    pe.wait_ge(S("y_kept"), at(1) - 8)

            with pe.Fori(0, 4) as s:
                steps(s, False)
            with pe.Fori(4, 8) as s:
                steps(s, True)

            pe.wait_ge(S("state_kept"), ZEROED + 4 * 8)
            pe.wait_ge(S("y_kept"), 8)
            pe.wait_ge(S("mod_kept"), 9)
            for j in range(NJ):
                pe.wait_ge(S("bonus_terms"), j + 1)
                mm(bank(j // 2)[:, (j % 2) * TX:(j % 2 + 1) * TX], cst("headones"), t4[:, j, :],
                   start=True, stop=True).then_inc(S("bonus_sums"), 1)
            pe.wait_ge(S("y_sum"), 1)
            for j in range(NJ):
                mm(bank(2 + j // 2)[:, (j % 2) * TX:(j % 2 + 1) * TX], cst("headones"), y[:, 0, j, :],
                   start=True, stop=True).then_inc(S("mean_sums"), 1)
            pe.wait_ge(S("gate_in"), 16)
            for j in range(NJ):
                mm(bank(4 + j // 2)[:, (j % 2) * TX:(j % 2 + 1) * TX], gate_w[:, j * P:(j + 1) * P], gd,
                   start=True, stop=True).then_inc(S("gates"), 1)
            for j in range(NJ):
                pe.wait_ge(S("y_squares"), j + 1)
                mm(bank(6 + j // 2)[:, (j % 2) * TX:(j % 2 + 1) * TX], cst("headones"), ysq[:, j, :],
                   start=True, stop=True).then_inc(S("var_sums"), 1)
            pe.wait_ge(S("y_scaled"), NJ)
            dense_product("wout", lambda kc: four[:, kc, :] if kc < NJ else rw[:, kc - NJ, :], TX,
                          wait_rhs=lambda kc: pe.wait_ge(S("rw_ready"), kc - NJ + 1) if kc >= NJ else None)

            norm_sums("norm2", sq2, KD, TX, 7)
            pe.wait_ge(S("wout_taken"), KD)
            dense_product("up", lambda kc: h2[:, kc, :], TX,
                          wait_rhs=lambda kc: pe.wait_ge(S("h2_ready"), kc + 1),
                          wait_bank=lambda e, j: e.wait_ge(S("ffn_taps"), 8 * (j + 1)))
            for half in range(2):
                if half == 1:
                    pe.wait_ge(S("ffn_taps"), 8 * 2 * NG)
                for q in range(3):
                    b = W_DOWN + 3 * half + q
                    have_block(pe, b)
                    for c in range(4):
                        for kc in range(block_rows(b)):
                            if half == 0 and c == 0:
                                pe.wait_ge(S("ffn_mul"), 8 * q + kc + 1)
                            last = mm(bank(4 * (1 - half) + c)[:, 0:TX], block_view(b)[:, kc, c * P:(c + 1) * P],
                                      g[:, 8 * q + kc, :], start=q == 0 and kc == 0,
                                      stop=q == 2 and kc == block_rows(b) - 1)
                        if q == 2 and c < 3:
                            last.then_inc(S("down"), 1)
                    last.then_inc(S("down_read"), 1)
            norm_sums("final1", sq2, KD, TX, 4)

            pe.wait_ge(S("consts2_in"), 16)
            norm_sums("gmix", sqV, KD, L, 7)

            def rotate_heads(j):
                e = j - QK_NORM
                if 0 <= e < 10:
                    pe.wait_ge(S("head_squares"), e + 1)
                    if e >= 1:
                        pe.wait_ge(S("head_roots"), e)
                    mm(bank(4)[:, 0:L], cst("ones"), sqq[e % 2], start=True, stop=True).then_inc(S("head_sums"), 1)
                e -= 3
                if 0 <= e < 10:
                    pe.wait_ge(S("qk_normed"), e + 1)
                    if e >= 2:
                        pe.wait_ge(S("qk_sined"), e - 1)
                    src = qb[:, e, :] if e < 8 else kb[:, e - 8, :]
                    mm(bank(5 + e % 2)[:, 0:L], cst2("rotate"), src, start=True, stop=True).then_inc(S("qk_turned"), 1)

            dense_product("proj2", lambda kc: u[:, kc, :], L,
                          wait_rhs=lambda kc: pe.wait_ge(S("gmix_norm"), kc + 1), after=rotate_heads)
            pe.wait_ge(S("proj2_taken"), 52)
            n = 0
            for e in range(10):
                if n >= 4:
                    pe.wait_ge(S("V_kept"), n - 3)
                src = va[:, e, :] if e < 8 else vb[:, e - 8, :]
                for t, (t0, nt) in enumerate(QC):
                    last = nc.tensor.transpose(bank(n % 4)[0:nt, t * P:(t + 1) * P], src[:, t0:t0 + nt], ident)
                last.then_inc(S("V_turned"), 1)
                n += 1
            def scores(n):
                un = units[n]
                q0, nq = QC[un.tile]
                if n == 0:
                    pe.wait_ge(S("V_kept"), 10)
                if n == 24:
                    pe.wait_ge(S("qk_rotated"), 10)
                if n >= 2:
                    pe.wait_ge(S("scores_read"), n - 1)
                for m in range(2):
                    if un.diff:
                        a, b = qa[64 * m:64 * m + 64, un.head, q0:q0 + nq], ka[64 * m:64 * m + 64, un.head, :]
                    else:
                        a, b = qb[:, un.head + m, q0:q0 + nq], kb[:, un.head // 4, :]
                    last = mm(bank(2 * (n % 2) + m)[0:nq, 0:L], a, b, start=True, stop=True)
                last.then_inc(S("scores"), 1)

            def turn_weights(n):
                un = units[n]
                q0, nq = QC[un.tile]
                for m in range(un.maps):
                    w = un.first_map + m
                    pe.wait_ge(S("weights"), w + 1)
                    if w >= 2:
                        pe.wait_ge(S("weights_kept"), 2 * (w - 1))
                    elif w == 0:
                        pe.wait_ge(S("qk_rotated"), 10)
                    for t, (t0, nt) in enumerate(QC):
                        last = nc.tensor.transpose(bank(4 + w % 2)[0:nt, t * P:t * P + nq], ee[n % 3][0:nq, m, t0:t0 + nt],
                                                   ident[0:nq, 0:nq])
                    last.then_inc(S("weights_turned"), 1)

            def weigh_values(n):
                un = units[n]
                for m in range(un.maps):
                    hd = un.out_head + m
                    pe.wait_ge(S("weights_kept"), 2 * (un.first_map + m + 1))
                    if hd >= 2:
                        pe.wait_ge(S("attended_kept"), hd - 1)
                    e = un.head if un.diff else 8 + un.head // 4
                    for t, (t0, nt) in enumerate(QC):
                        last = mm(bank(6 + hd % 2)[:, 0:L], V[0:nt, t, e, :], WT[hd % 2][0:nt, t, :], start=t == 0,
                                  stop=t == 2)
                    last.then_inc(S("attended"), 1)

            for n in range(len(units) + 4):
                if n < len(units):
                    scores(n)
                if 3 <= n <= len(units) + 2:
                    turn_weights(n - 3)
                if n >= 4 and units[n - 4].tile == 2:
                    weigh_values(n - 4)
            def head_sum(e):
                pe.wait_ge(S("head_squares"), 10 + e + 1)
                if e >= 1:
                    pe.wait_ge(S("head_roots"), 10 + e)
                mm(bank(4)[:, 0:L], cst("ones"), sqq[e % 2], start=True, stop=True).then_inc(S("head_sums"), 1)

            pe.wait_ge(S("attended_kept"), 16)
            dense_product("branch_b", lambda kc: ob[:, kc, :], L, after=head_sum)
            pe.wait_ge(S("branch_b_taken"), KD)
            dense_product("branch_a", lambda kc: oa[:, kc, :], L,
                          wait_rhs=lambda kc: pe.wait_ge(S("oa_normed"), kc + 1),
                          wait_bank=lambda e, j: e.wait_ge(S("branch_a_steps"), 2 * (j + 1)))
            pe.wait_ge(S("branch_a_steps"), 2 * KD)
            dense_product("wout2", lambda kc: ga[:, kc, :], L)
            norm_sums("gffn", sqq8, KD, L, 7)
            pe.wait_ge(S("wout2_taken"), KD)

            pe.wait_ge(S("router_in"), 16)
            pe.wait_ge(S("gffn_norm"), KD)
            for t, (t0, nt) in enumerate(QC):
                for kc in range(KD):
                    last = mm(bank(0)[0:nt, t * NE:(t + 1) * NE], u[:, kc, t0:t0 + nt], router[:, kc, :],
                              start=kc == 0, stop=kc == KD - 1)
            last.then_inc(S("logits"), 1)
            for c in range(KD):
                if c >= 2:
                    pe.wait_ge(S("utok_kept"), c - 1)
                for t, (t0, nt) in enumerate(QC):
                    last = nc.tensor.transpose(bank(1 + c % 2)[0:nt, t * P:(t + 1) * P], u[:, c, t0:t0 + nt], ident)
                last.then_inc(S("u_turned"), 1)
            pe.wait_ge(S("aff"), 1)
            for t, (t0, nt) in enumerate(QC):
                last = nc.tensor.transpose(bank(3)[0:NE, t0:t0 + nt], aff[0:nt, t, :], ident[0:nt, 0:nt])
            last.then_inc(S("aff_turned"), 1)
            pe.wait_ge(S("places"), 1)
            for t, (t0, nt) in enumerate(QC):
                last = nc.tensor.transpose(bank(4)[0:nt, t * NE:(t + 1) * NE], places[0:NE, t0:t0 + nt],
                                           ident[0:NE, 0:NE])
            last.then_inc(S("places_turned"), 1)
            for i in range(NE // 2):
                pe.wait_ge(S("selA_ready"), 1)
                if i >= 2:
                    pe.wait_ge(S("selT_kept"), i - 1)
                for t, (t0, nt) in enumerate(QC):
                    last = nc.tensor.transpose(bank(5 + i % 2)[:, t0:t0 + nt],
                                               selA[0:nt, t, 2 * i:2 * i + 2, :].rearrange("p e s -> p (e s)"),
                                               ident[0:nt, 0:nt])
                last.then_inc(S("selT"), 1)
            pe.wait_ge(S("selT_kept"), NE // 2)
            pe.wait_ge(S("utok_kept"), KD)

            sel_flat = sel.rearrange("p t e s -> p t (e s)")

            def gather(i):
                for half in range(2):
                    for c in range(4):
                        for t, (t0, nt) in enumerate(QC):
                            last = mm(bank(half)[:, c * P:(c + 1) * P],
                                      utok[0:nt, t, (4 * half + c) * P:(4 * half + c + 1) * P],
                                      sel_flat[0:nt, t, bass.ds(i * P, P)], start=t == 0, stop=t == 2)
                    last.then_inc(S("gathered"), 1)

            def pair(i, more):
                pe.wait_ge(S("xs_kept"), 2 * i + 2)
                for name, b, s in (("gate", 2, 0), ("up_e", 3, 2)):
                    for e in range(2):
                        pe.wait_ge(S("eslot%d" % (s + e)), 16 * (i + 1))
                        w = eslots[s + e].rearrange("p (k c) -> p k c", k=KD)
                        for kc in range(KD):
                            last = mm(bank(b)[64 * e:64 * e + 64, :], xsT[:, kc, 64 * e:64 * e + 64], w[:, kc, :],
                                      start=kc == 0, stop=kc == KD - 1)
                    last.then_inc(S(name), 1)
                if more:
                    gather(i + 1)
                pe.wait_ge(S("hid"), i + 1)
                for f in range(4):
                    last = nc.tensor.transpose(bank(2)[:, f * P:(f + 1) * P], hid[:, f * P:(f + 1) * P], ident)
                last.then_inc(S("hid_turned"), 1)
                pe.wait_ge(S("hidT"), i + 1)
                for half in range(2):
                    for e in range(2):
                        pe.wait_ge(S("eslot%d" % (4 + e)), 16 * (i + 1))
                        w = eslots[4 + e].rearrange("p (k c) -> p k c", k=4)
                        for f in range(4):
                            last = mm(bank(4 + half)[64 * e:64 * e + 64, :], hidT[:, f, 64 * e:64 * e + 64],
                                      w[:, f, half * 512:(half + 1) * 512], start=f == 0, stop=f == 3)
                    last.then_inc(S("down_e"), 1)
                for c in range(KD):
                    pe.wait_ge(S("y_e"), 2 * i + 1 + c // 4)
                    if c >= 2:
                        pe.wait_ge(S("added"), i * KD + c - 1)
                    mm(bank(6 + c % 2)[:, 0:L], yexp[:, c * P:(c + 1) * P], selT[:, bass.ds(i, 1), :]
                       .rearrange("p o t -> p (o t)"), start=True, stop=True).then_inc(S("spread"), 1)
                pe.wait_ge(S("added"), i * KD + KD)

            gather(0)
            with pe.Fori(0, NE // 2 - 1) as i:
                pair(i, True)
            pair(NE // 2 - 1, False)
            norm_sums("last", sqq8, KD, L, 0)

        def token_at(s, d, outputs):
            return s * C if d == 0 else s * -C + ((TB + TC - C) if outputs else (TC - C))

        def bc(ap, *shape):
            return ap.to_broadcast(list(shape))

        def per_channel(cols, n, width):
            return bc(cols.rearrange("p (n o) -> p n o", o=1), P, n, width)

        def four_chunks(b):
            return ps[:, b:b + 2, :].rearrange("p b (q t) -> p (b q) t", q=2)

        def by_pair(b, width):
            return bank(b)[:, 0:NJ * width].rearrange("p (j c) -> p j c", j=NJ)

        @block.scalar
        def _(act):
            A = nc.scalar.activation
            act.dma_start(params, dram["params"]).then_inc(S("params_in"), 16)
            act.dma_start(decay_w.rearrange("p d c -> p (d c)"), dram["decay_w2"]).then_inc(S("lora_in"), 16)
            act.dma_start(iclr_w.rearrange("p d c -> p (d c)"), dram["iclr_a2"]).then_inc(S("lora_in"), 16)
            act.dma_start(gate_w, dram["gate_g2"]).then_inc(S("gate_in"), 16)

            def norm(name, src, sq, chunks, n, b, rt, eps, wait=None, width=D):
                for c in range(chunks):
                    if wait:
                        wait(c)
                    A(sq[:, c, 0:n], src[:, c, 0:n], ACT.Square).then_inc(S("norm_squares"), 1)
                act.wait_ge(S("norm_sums"), NORMS[name][0] + 1)
                A(rt[:, 0:n], bank(b)[:, 0:n], ACT.Sqrt, scale=1.0 / width, bias=eps).then_inc(S("norm_roots"), 1)

            act.wait_ge(S("cond_in"), 16)
            A(cond_act, cond, ACT.Silu).then_inc(S("cond_act"), 1)
            act.wait_ge(S("tokens_in"), 16)
            norm("norm1", tokens, squares, KD, TB, 7, root, EPS)
            for n in range(W_IN):
                act.wait_ge(S("mod_rows"), n + 1)
                if n >= 2:
                    act.wait_ge(S("mod_turned"), n - 1)
                A(mod_rows[0:2, n % 2, :], bank(n % 2)[0:2, :], ACT.Copy).then_inc(S("mod_rows_kept"), 1)
            for c in range(KD):
                for half in range(2):
                    act.wait_ge(S("h_scaled"), 2 * c + half + 1)
                    x = h[:, c, half * TC:(half + 1) * TC]
                    A(x, x, ACT.Identity, bias=mod[:, c, 1 - half:2 - half]).then_inc(S("h_ready"), 1)
            for j in range(19):
                act.wait_ge(S("proj"), j + 1)
                b = bank(j % 4)
                if j < 4:
                    A(four[:, j, :], b[:, 0:TX], ACT.Copy).then_inc(S("proj_taken"), 1)
                elif j < 16:
                    dst = r[:, j - 4, :] if j < 8 else k[:, j - 8, :] if j < 12 else v[:, j - 12, :]
                    n = TX if j < 8 else TB
                    A(dst, b[:, 0:n], ACT.Copy, scale=prm("conv", 12 + j - 4)).then_inc(S("conv_mid"), 1)
                elif j == 16:
                    A(wd, b, ACT.Tanh).then_inc(S("proj_taken"), 1)
                elif j == 17:
                    A(ad, b, ACT.Copy).then_inc(S("proj_taken"), 1)
                else:
                    A(gd, b[:, 0:TX], ACT.Sigmoid).then_inc(S("proj_taken"), 1)
            for j in range(NJ):
                act.wait_ge(S("kk_scaled"), j + 1)
                if j >= 2:
                    act.wait_ge(S("kk_sums"), j - 1)
                A(kk_sq[:, j % 2, :], kk[:, j, :], ACT.Square).then_inc(S("kk_squares"), 1)
            for j in range(NJ):
                act.wait_ge(S("kk_sums"), j + 1)
                A(kk_root[:, j, :], bank(4 + j), ACT.Sqrt, bias=KK_EPS).then_inc(S("kk_root"), 1)
            n = 0
            for dst, base in ((cum_before, "w0"), (iclr, "a0")):
                for d in range(2):
                    for j in range(NJ):
                        act.wait_ge(S("lora"), n + 1)
                        A(dst[:, d, j, :], bank(4 + n % 2), ACT.Sigmoid, bias=prm(base, NJ * d + j))\
                            .then_inc(S("lora_taken"), 1)
                        n += 1
            for n in range(4):
                act.wait_ge(S("spectrum"), n + 1)
                t, jj = n // 2, n % 2
                A(spectrum[:, t, 2 * jj:2 * jj + 2, :], bank(6 + n % 2).rearrange("p (q c) -> p q c", q=2), ACT.Copy)\
                    .then_inc(S("spectrum_kept"), 1)
            for jj in range(2):
                act.wait_ge(S("mixed"), jj + 1)
                A(four[:, 2 * jj:2 * jj + 2, :], bank(6 + jj).rearrange("p (q c) -> p q c", q=2), ACT.Copy)\
                    .then_inc(S("mixed_kept"), 1)
            act.wait_ge(S("mixed_kept"), 2)
            act.wait_ge(S("kk_recip"), NJ)
            norm("four", four, squares_f, NJ, TX, 6, root, EPS, width=FW)

            def decays(s, outputs, ahead):
                for d in range(2):
                    t = token_at(s, d, outputs) + (ahead * C if d == 0 else -ahead * C)
                    A(EC[d], cum[:, d, :, bass.ds(t, C)], ACT.Exp, scale=-LOG_DECAY)
                    A(EP[d], cum_before[:, d, :, bass.ds(t, C)], ACT.Exp, scale=-LOG_DECAY)
                    A(EI[d], cum[:, d, :, bass.ds(t, C)], ACT.Exp, scale=LOG_DECAY).then_inc(S("decays"), 1)

            def steps(s, outputs, next_outputs):
                at = lambda d: 2 * s + d + 1

                def keep_piece(piece):
                    act.wait_ge(S("mod_rows"), 2 * s + (W_IN + piece + 1))
                    act.wait_ge(S("mod_turned"), 2 * s + W_IN)
                    A(late_rows[0:2, piece, :], bank(7)[0:2, 256:256 + PIECE], ACT.Copy).then_inc(S("mod_rows_kept"), 1)

                keep_piece(0)

                def keep(name, b, dst, *waits, scale=1.0):
                    for d in range(2):
                        act.wait_ge(*turn(name, s, d))
                        for w in waits:
                            act.wait_ge(*turn(w, s, d))
                        A(dst[d], by_pair(4 * d + b, P), ACT.Copy, scale=scale).then_inc(turns_of(name + "_kept"), 1)

                for d in range(2):
                    act.wait_ge(*turn("keys_turned", s, d))
                    A(KBT[d], by_pair(4 * d, P), ACT.Copy, scale=cst("sign")).then_inc(turns_of("keys_kept"), 1)
                for d in range(2):
                    act.wait_ge(*turn("values_turned", s, d))
                    A(VU[d][0:64, :, :], by_pair(4 * d + 1, P)[0:64, :, :], ACT.Copy).then_inc(turns_of("values_kept"), 1)
                keep("A2", 2, B3)
                keep("A2T", 3, B4)
                keep("A4", 0, B1, "Q0_kept")
                keep("inverse8", 3, B2)
                keep("M", 0, B3)
                keep("MT", 1, B4)
                keep("M2", 2, B1)
                keep("M2T", 3, B5)
                keep("M4", 1, B2)
                act.wait_ge(S("reads_staged"), 4 * s + 4)
                if outputs:
                    act.wait_ge(S("outs_staged"), 4 * s - 12)
                act.wait_ge(S("keys_staged"), 16 * s + 16)
                if next_outputs is not None:
                    decays(s, next_outputs, 1)
                for d in range(2):
                    act.wait_ge(*turn("held", s, d))
                    A(X[d], by_pair(4 * d + 3, C), ACT.Copy).then_inc(turns_of("held_kept"), 1)
                keep_piece(1)
                for d in range(2):
                    act.wait_ge(*turn("removed", s, d))
                    A(VU[d][64:128, :, :].rearrange("p j (h c) -> p h j c", h=2),
                      ps[64:128, 4 * d + 1:4 * d + 3, 0:NJ * C].rearrange("p h (j c) -> p h j c", j=NJ), ACT.Copy).then_inc(turns_of("removed_kept"), 1)
                if outputs:
                    for d in range(2):
                        act.wait_ge(S("y_made"), at(d) - 8)
                        t = s * C - TC if d == 0 else s * -C + (TB - C)
                        A(y[:, d, :, bass.ds(t, C)], by_pair(4 * d + 3, C), ACT.Copy).then_inc(S("y_kept"), 1)
                act.wait_ge(S("mod_turned"), 2 * s + (W_IN + 2))
                A(mod[:, bass.ds(4 * s + 16, 4), :], bank(3)[:, 256:264].rearrange("p (n o) -> p n o", o=2), ACT.Copy)\
                    .then_inc(S("mod_kept"), 1)

            act.wait_ge(S("sums_before"), 2)
            decays(0, False, 0)
            with act.Fori(0, 3) as s:
                steps(s, False, False)
            steps(3, False, True)
            with act.Fori(4, 7) as s:
                steps(s, True, True)
            steps(7, True, None)

            for j in range(NJ):
                act.wait_ge(S("y_centred"), j + 1)
                A(ysq[:, j, :], y[:, 0, j, :], ACT.Square).then_inc(S("y_squares"), 1)
            for j in range(NJ):
                act.wait_ge(S("var_sums"), j // 2 * 2 + 2)
                A(y[:, 1, j, :], four_chunks(6)[:, j, :], ACT.Sqrt, scale=1.0 / HEAD, bias=GN_EPS)\
                    .then_inc(S("var_root"), 1)

            norm("norm2", xres, sq2, KD, TX, 7, root, EPS, wait=lambda c: act.wait_ge(S("wout_taken"), c + 1))
            for c in range(KD):
                act.wait_ge(S("h2_scaled"), c + 1)
                A(h2[:, c, :], h2[:, c, :], ACT.Identity, bias=mod[:, 24 + c, 0:1]).then_inc(S("h2_ready"), 1)

            def activate_gate(j):
                act.wait_ge(S("ffn_taps"), 8 * (j + 1))
                A(g[:, j, :], g[:, j, :], ACT.Silu).then_inc(S("ffn_act"), 1)

            for j in range(2 * NG):
                act.wait_ge(S("up"), j + 1)
                if j >= NG + 2:
                    act.wait_ge(S("ffn_mul"), j - NG - 1)
                dst = g[:, j, :] if j < NG else acc[:, j % 2, :]
                A(dst, bank(j % 4)[:, 0:TX], ACT.Identity, scale=prm("ffn_conv", 4 * 2 * NG + j),
                  bias=prm("ffn_b", j)).then_inc(S("ffn_mid"), 1)
                if 1 <= j <= NG:
                    activate_gate(j - 1)
            norm("final1", xres, sq2, KD, TX, 4, root, EPS, wait=lambda c: act.wait_ge(S("down_taken"), c + 1))

            norm("gmix", H, sqV, KD, L, 7, rt2, EPS,
                 wait=lambda c: (act.wait_ge(S("H_ready"), c + 1), act.wait_ge(S("meta_in"), 16)))

            def head_square(name, e, head):
                if e >= 2:
                    act.wait_ge(S("head_sums"), HEAD_NORMS[name] + e - 1)
                A(sqq[e % 2], head, ACT.Square).then_inc(S("head_squares"), 1)

            def head_root(name, e, width=P):
                act.wait_ge(S("head_sums"), HEAD_NORMS[name] + e + 1)
                if e >= 1:
                    act.wait_ge(S("head_recips"), HEAD_NORMS[name] + e)
                A(rt2, bank(4)[:, 0:L], ACT.Sqrt, scale=1.0 / width, bias=EPS).then_inc(S("head_roots"), 1)

            act.wait_ge(S("lam_sums"), 2)
            for j in range(52):
                e = j - QK_NORM
                if 0 <= e < 10:
                    if e == 0:
                        act.wait_ge(S("proj2_taken"), 36)
                    head_square("qk", e, qb[:, e, :] if e < 8 else kb[:, e - 8, :])
                act.wait_ge(S("proj2"), j + 1)
                dst = (qa[:, j, :] if j < 8 else ka[:, j - 8, :] if j < 16 else va[:, j - 16, :] if j < 24
                       else qb[:, j - 24, :] if j < 32 else kb[:, j - 32, :] if j < 34 else vb[:, j - 34, :] if j < 36
                       else ga[:, j - 36, :] if j < 44 else gb[:, j - 44, :])
                A(dst, bank(j % 4)[:, 0:L], ACT.Sigmoid if j >= 36 else ACT.Copy).then_inc(S("proj2_taken"), 1)
                if 0 <= e < 10:
                    head_root("qk", e)

            A(lam_s[:, 2:4], lam_s[:, 0:2], ACT.Exp).then_inc(S("lam_exp"), 1)

            def exponentials(n):
                un = units[n]
                nq = QC[un.tile][1]
                act.wait_ge(S("maxima"), n + 1)
                if n >= 3:
                    p = units[n - 3]
                    act.wait_ge(S("weights_turned"), p.first_map + p.maps)
                scale = HEAD ** -0.5 if un.diff else P ** -0.5
                for m in range(2):
                    src = sc[n % 2][0:nq, m, :] if un.diff else bank(2 * (n % 2) + m)[0:nq, 0:L]
                    last = A(ee[n % 3][0:nq, m, :], src, ACT.Exp, scale=scale, bias=stat[n % 3][0:nq, 2 + m:3 + m],
                             accum_out=stat[n % 3][0:nq, 4 + m:5 + m])
                last.then_inc(S("scores_read"), 1)

            def keep_weights(n):
                un = units[n]
                q0, nq = QC[un.tile]
                for m in range(un.maps):
                    w = un.first_map + m
                    buf = WT[(un.out_head + m) % 2]
                    act.wait_ge(S("weights_turned"), w + 1)
                    if un.tile == 0 and un.out_head + m >= 2:
                        act.wait_ge(S("attended"), un.out_head + m - 1)
                    b = bank(4 + w % 2)
                    A(buf[:, 0:2, q0:q0 + nq], b[:, 0:2 * P].rearrange("p (t q) -> p t q", t=2)[:, :, 0:nq], ACT.Copy)\
                        .then_inc(S("weights_kept"), 1)
                    A(buf[0:16, 2, q0:q0 + nq], b[0:16, 2 * P:2 * P + nq], ACT.Copy).then_inc(S("weights_kept"), 1)

            def keep_attended(n):
                un = units[n]
                for m in range(un.maps):
                    hd = un.out_head + m
                    act.wait_ge(S("attended"), hd + 1)
                    dst = oa[:, hd, :] if un.diff else ob[:, hd - AH, :]
                    A(dst, bank(6 + hd % 2)[:, 0:L], ACT.Copy).then_inc(S("attended_kept"), 1)

            for n in range(len(units) + 4):
                if n < len(units):
                    exponentials(n)
                if 3 <= n <= len(units) + 2:
                    keep_weights(n - 3)
                if n >= 4 and units[n - 4].tile == 2:
                    keep_attended(n - 4)
            act.wait_ge(S("attended_kept"), 16)
            for e in range(AH + 1):
                if e < AH:
                    head_square("oa", e, oa[:, e, :])
                if e >= 1:
                    head_root("oa", e - 1)
            norm("gffn", H, sqq8, KD, L, 7, rt2, EPS, wait=lambda c: act.wait_ge(S("wout2_taken"), c + 1))

            act.wait_ge(S("logits_shifted"), 2)
            for rows, t0, t1 in ((P, 0, 2), (16, 2, 3)):
                A(aff[0:rows, t0:t1, :], logit[0:rows, t0:t1, :], ACT.Exp).then_inc(S("logits_exp"), 1)
            for c in range(KD):
                act.wait_ge(S("u_turned"), c + 1)
                b = bank(1 + c % 2)
                A(utok[:, 0:2, c * P:(c + 1) * P], b[:, 0:2 * P].rearrange("p (t q) -> p t q", t=2), ACT.Copy)
                A(utok[0:16, 2, c * P:(c + 1) * P], b[0:16, 2 * P:3 * P], ACT.Copy).then_inc(S("utok_kept"), 1)
            for i in range(NE // 2):
                act.wait_ge(S("selT"), i + 1)
                act.wait_ge(S("places_turned"), 1)
                A(selT[:, i, :], bank(5 + i % 2)[:, 0:L], ACT.Copy).then_inc(S("selT_kept"), 1)

            def keep_gathered(i):
                for half in range(2):
                    act.wait_ge(S("gathered"), 2 * i + half + 1)
                    A(xsT[:, 4 * half:4 * half + 4, :], bank(half).rearrange("p (c s) -> p c s", c=4), ACT.Copy)\
                        .then_inc(S("xs_kept"), 1)

            def pair(i, more):
                act.wait_ge(S("gate"), i + 1)
                A(hgate, bank(2), ACT.Silu).then_inc(S("silu"), 1)
                if more:
                    act.wait_ge(S("up_e"), i + 1)
                    keep_gathered(i + 1)
                act.wait_ge(S("hid_turned"), i + 1)
                A(hidT, bank(2).rearrange("p (f s) -> p f s", f=4), ACT.Copy).then_inc(S("hidT"), 1)
                for half in range(2):
                    act.wait_ge(S("down_e"), 2 * i + half + 1)
                    A(yexp[:, half * 512:(half + 1) * 512], bank(4 + half), ACT.Copy).then_inc(S("y_e"), 1)
                act.wait_ge(S("hid"), i + 1)

            keep_gathered(0)
            with act.Fori(0, NE // 2 - 1) as i:
                pair(i, True)
            pair(NE // 2 - 1, False)
            norm("last", H, sqq8, KD, L, 0, rt2, EPS,
                 wait=lambda c: act.wait_ge(S("added"), NE // 2 * KD))

        @block.vector
        def _(dve):
            V_ = nc.vector
            tt, stt, ts = V_.tensor_tensor, V_.scalar_tensor_tensor, V_.tensor_scalar

            def apply_norm(name, src, dst, n, rt, rs, gain, done, chunks=KD):
                dve.wait_ge(*norm_root(name))
                V_.reciprocal(rs[:, 0:n], rt[:, 0:n]).then_inc(S("norm_recips"), 1)
                dve.wait_ge(S("norm_recips"), NORMS[name][0] + 1)
                for c in range(chunks):
                    stt(out=dst[:, c, :], in0=src[:, c, :], scalar=gain(c), in1=rs[:, 0:n], op0=ALU.mult,
                        op1=ALU.mult).then_inc(S(done), 1)

            dve.wait_ge(S("params_in"), 16)
            ts(ka_rest, prm("k_a", 0, NJ), -1.0, 1.0, ALU.mult, ALU.add)
            ts(ka_rest2, prm("k_a", 0, NJ), -2.0, 2.0, ALU.mult, ALU.add).then_inc(S("ka_rest"), 1)
            dve.wait_ge(*norm_root("norm1"))
            V_.reciprocal(rstd, root).then_inc(S("norm_recips"), 1)
            dve.wait_ge(S("mod_turned"), W_IN)
            tt(mod[:, 0:16, :], bank(2)[:, 0:32].rearrange("p (n o) -> p n o", o=2), per_channel(prm("ada_b", 0, 16), 16, 2),
               ALU.add).then_inc(S("mod_kept"), 1)
            dve.wait_ge(S("mod_kept"), 1)
            stt(out=coef1, in0=mod[:, 8:16, :], scalar=1.0, in1=per_channel(prm("norm1_g", 0, KD), KD, 2),
                op0=ALU.add, op1=ALU.mult).then_inc(S("coefs"), 1)
            dve.wait_ge(S("coefs"), 1)
            dve.wait_ge(S("norm_recips"), 1)
            for c in range(KD):
                for half in range(2):
                    t = slice(half * TC, (half + 1) * TC)
                    stt(out=h[:, c, t], in0=tokens[:, c, t], scalar=coef1[:, c, 1 - half:2 - half], in1=rstd[:, t],
                        op0=ALU.mult, op1=ALU.mult).then_inc(S("h_scaled"), 1)
            for q in range(12):
                n_seq = 1 if q < 4 else 2
                dst = r[:, q, :] if q < 4 else k[:, q - 4, :] if q < 8 else v[:, q - 8, :]
                dst = dst.rearrange("p (n t) -> p n t", n=n_seq)
                src = bank((q + 4) % 4)[:, 0:n_seq * TX].rearrange("p (n t) -> p n t", n=n_seq)
                dve.wait_ge(S("conv_mid"), q + 1)
                stt(out=dst[:, :, 1:TX], in0=src[:, :, 0:TX - 1], scalar=prm("conv", q), in1=dst[:, :, 1:TX],
                    op0=ALU.mult, op1=ALU.add).then_inc(S("conv_steps"), 1)
                dve.wait_ge(S("conv_steps"), 2 * q + 1)
                stt(out=dst[:, :, 0:TX - 1], in0=src[:, :, 1:TX], scalar=prm("conv", 24 + q), in1=dst[:, :, 0:TX - 1],
                    op0=ALU.mult, op1=ALU.add).then_inc(S("conv_steps"), 1)
            dve.wait_ge(S("conv_steps"), 24)
            for j in range(NJ):
                ts(kk[:, j, :], k[:, j, :], prm("k_k", j), None, ALU.mult).then_inc(S("kk_scaled"), 1)
            for j in range(NJ):
                dve.wait_ge(S("kk_root"), j + 1)
                if j >= 1:
                    dve.wait_ge(S("kk_unit"), j)
                V_.reciprocal(rstd, kk_root[:, j, :]).then_inc(S("kk_recip"), 1)
                dve.wait_ge(S("kk_recip"), j + 1)
                tt(kk[:, j, :], kk[:, j, :], rstd, ALU.mult).then_inc(S("kk_unit"), 1)
            dve.wait_ge(S("kk_unit"), NJ)
            apply_norm("four", four, four, TX, root, rstd, lambda c: prm("fourier_g", c), "four_norm", NJ)
            for d in range(2):
                dve.wait_ge(S("lora_taken"), 16)
                for j in range(NJ):
                    x, o, keep = cum_before[:, d, j, :], cum[:, d, j, :], cst("keep%d" % d)
                    if d == 1:
                        x, o, keep = x[:, ::-1], o[:, ::-1], keep[:, ::-1]
                    last = V_.tensor_tensor_scan(o, keep, x, 0.0, ALU.mult, ALU.add)
                last.then_inc(S("sums"), 1)
            dve.wait_ge(S("proj"), 19)
            dve.wait_ge(S("four_norm"), NJ)
            for d in range(2):
                V_.memset(ST[d], 0.0).then_inc(S("state_kept"), 1)
                V_.memset(KR[d], 0.0).then_inc(S("state_kept"), 1)
                V_.memset(VU[d][64:128, :, :], 0.0).then_inc(S("state_kept"), 1)
            dve.wait_ge(S("state_kept"), ZEROED)

            def steps(s, outputs):
                at = lambda d: 2 * s + d + 1
                for d in range(2):
                    t = token_at(s, d, outputs)
                    dve.wait_ge(S("decays"), at(d))
                    last_token = EC[d][:, :, C - 1:C] if d == 0 else EC[d][:, :, 0:1]
                    tt(EW[d], bc(last_token, P, NJ, P), bc(cst("headones").rearrange("p (o c) -> p o c", o=1), P, NJ, P),
                       ALU.mult)
                    for p in range(2):
                        hp = slice(64 * p, 64 * p + 64)
                        tt(KR[d][hp, :, 0, p, :], kk[hp, :, bass.ds(t, C)], EP[d][hp, :, :], ALU.mult)\
                            .then_inc(S("reads_staged"), 1)
                        if outputs:
                            tt(KR[d][hp, :, 1, p, :], r[hp, :, bass.ds(t - TC, C)], EC[d][hp, :, :], ALU.mult)\
                                .then_inc(S("outs_staged"), 1)
                na = 2 if outputs else 1
                for q in range(2):
                    for d in range(2):
                        dve.wait_ge(*turn("gram%d" % q, s, d))
                        mask = bc(cst("gram%d" % d)[:, 0:na * P].rearrange("p (o c) -> p o c", o=1), P, 2, na * P)
                        tt(GM[d][:, 2 * q:2 * q + 2, 0:na, :, :].rearrange("p j a h c -> p j (a h c)"),
                           bank(4 * d + q).rearrange("p (j c) -> p j c", j=2)[:, :, 0:na * P], mask, ALU.mult)\
                            .then_inc(turns_of("gram%d_kept" % q), 1)
                for d in range(2):
                    dve.wait_ge(*turn("removalsT", s, d))
                    for dst, name, b in ((B1, "diagT%d", 2), (B5, "offT%d", 2), (B2, "diag%d", 3)):
                        if b == 3:
                            dve.wait_ge(*turn("removals", s, d))
                        last = tt(dst[d], by_pair(4 * d + b, P), bc(cst(name % d).rearrange("p (o c) -> p o c", o=1), P, NJ, P),
                                  ALU.mult)
                    last.then_inc(turns_of("A_kept"), 1)
                for d in range(2):
                    dve.wait_ge(*turn("A_kept", s, d))
                    tt(Q[d], B1[d], bc(ident.rearrange("p (o c) -> p o c", o=1), P, NJ, P), ALU.add)\
                        .then_inc(turns_of("Q0_kept"), 1)
                before = "Q0_kept"
                for name, b in (("Q1", 1), ("Q2", 2), ("R1", 0), ("R2", 2), ("R3", 0)):
                    for d in range(2):
                        dve.wait_ge(*turn(name, s, d))
                        dve.wait_ge(*turn(before, s, d))
                        tt(Q[d], by_pair(4 * d + b, P), Q[d], ALU.add).then_inc(turns_of(name + "_kept"), 1)
                    before = name + "_kept"
                for d in range(2):
                    dve.wait_ge(*turn("state_made", s, d))
                    if outputs:
                        dve.wait_ge(S("y_made"), at(d) - 8)
                    tt(ST[d], by_pair(4 * d, P), ST[d], ALU.add).then_inc(S("state_kept"), 1)
                dve.wait_ge(S("state_kept"), 4 * s + (ZEROED + 2))
                for d in range(2):
                    tt(ST[d], ST[d], EW[d], ALU.mult).then_inc(S("state_kept"), 1)
                dve.wait_ge(S("state_kept"), 4 * s + (ZEROED + 4))

            with dve.Fori(0, 4) as s:
                steps(s, False)
            with dve.Fori(4, 8) as s:
                steps(s, True)

            n = Tally(S("mix_steps"))
            n(tt(t4, iclr[:, 0, :, TC:TB], iclr[:, 1, :, TC:TB], ALU.add))
            n.wait(dve)
            for j in range(NJ):
                n(ts(t4[:, j, :], t4[:, j, :], prm("k_a", j), ka_rest2[:, j:j + 1], ALU.mult, ALU.add))
            n.wait(dve)
            n(tt(t4, t4, k[:, :, TC:TB], ALU.mult))
            n.wait(dve)
            for j in range(NJ):
                stt(out=t4[:, j, :], in0=t4[:, j, :], scalar=prm("r_k", j), in1=r[:, j, :], op0=ALU.mult, op1=ALU.mult)\
                    .then_inc(S("bonus_terms"), 1)
            dve.wait_ge(S("y_kept"), 8)
            tt(y[:, 0, :, :], y[:, 0, :, :], y[:, 1, :, :], ALU.add).then_inc(S("y_sum"), 1)
            dve.wait_ge(S("mod_kept"), 9)
            tt(mod[:, 16:48, :], mod[:, 16:48, :], per_channel(prm("ada_b", 16, 32), 32, 2), ALU.add)\
                .then_inc(S("coefs"), 1)
            dve.wait_ge(S("coefs"), 2)
            stt(out=coef2, in0=mod[:, 32:40, 0], scalar=1.0, in1=prm("norm2_g", 0, KD), op0=ALU.add,
                op1=ALU.mult).then_inc(S("coefs"), 1)
            dve.wait_ge(S("mean_sums"), NJ)
            dve.wait_ge(S("y_sum"), 1)
            for j in range(NJ):
                stt(out=y[:, 0, j, :], in0=four_chunks(2)[:, j, :], scalar=-1.0 / HEAD, in1=y[:, 0, j, :], op0=ALU.mult,
                    op1=ALU.add).then_inc(S("y_centred"), 1)
            dve.wait_ge(S("bonus_sums"), NJ)
            n(tt(bonus, four_chunks(0), v[:, :, TC:TB], ALU.mult))
            n.wait(dve)
            for j in range(NJ):
                n(ts(bonus[:, j, :], bonus[:, j, :], prm("gn_b", j), None, ALU.add))
            for j in range(NJ):
                dve.wait_ge(S("var_root"), j + 1)
                n(V_.reciprocal(y[:, 1, j, :], y[:, 1, j, :]))
            for j in range(NJ):
                dve.wait_ge(S("mix_steps"), n.n - NJ + j + 1)
                stt(out=y[:, 0, j, :], in0=y[:, 0, j, :], scalar=prm("gn_g", j), in1=y[:, 1, j, :], op0=ALU.mult,
                    op1=ALU.mult).then_inc(S("y_scaled"), 1)
            dve.wait_ge(S("y_scaled"), NJ)
            n(tt(y[:, 0, :, :], y[:, 0, :, :], bonus, ALU.add))
            n.wait(dve)
            dve.wait_ge(S("gates"), NJ)
            for j in range(NJ):
                tt(rw[:, j, :], four_chunks(4)[:, j, :], y[:, 0, j, :], ALU.mult).then_inc(S("rw_ready"), 1)

            for c in range(KD):
                dve.wait_ge(S("wout"), c + 1)
                stt(out=xres[:, c, :], in0=bank(c % 4)[:, 0:TX], scalar=mod[:, 16 + c, 0:1], in1=xres[:, c, :],
                    op0=ALU.mult, op1=ALU.add).then_inc(S("wout_taken"), 1)
            apply_norm("norm2", xres, h2, TX, root, rstd, lambda c: coef2[:, c:c + 1], "h2_scaled")
            n = Tally(S("ffn_taps"))
            for j in range(2 * NG):
                dst = (g[:, j, :] if j < NG else acc[:, j % 2, :]).rearrange("p (r c) -> p r c", r=ROWS)
                src = bank(j % 4)[:, 0:TX].rearrange("p (r c) -> p r c", r=ROWS)
                dve.wait_ge(S("ffn_mid"), j + 1)
                for tap in range(9):
                    if tap == 4:
                        continue
                    dy, dx = tap // 3 - 1, tap % 3 - 1
                    r0, r1 = max(0, -dy), ROWS - max(0, dy)
                    c0, c1 = max(0, -dx), GRID - max(0, dx)
                    o = dst[:, r0:r1, c0:c1]
                    if tap > 0:
                        n.wait(dve)
                    n(stt(out=o, in0=src[:, r0 + dy:r1 + dy, c0 + dx:c1 + dx],
                          scalar=prm("ffn_conv", tap * 2 * NG + j), in1=o, op0=ALU.mult, op1=ALU.add))
            for c in range(KD):
                half, q = c // 4, c % 4
                if q < 3:
                    dve.wait_ge(S("down"), 3 * half + q + 1)
                else:
                    dve.wait_ge(S("down_read"), 3 * half + 3)
                stt(out=xres[:, c, :], in0=bank(4 * (1 - half) + q)[:, 0:TX], scalar=mod[:, 40 + c, 0:1], in1=xres[:, c, :],
                    op0=ALU.mult, op1=ALU.add).then_inc(S("down_taken"), 1)
            apply_norm("final1", xres, H[:, :, META:L], TX, root, rstd, lambda c: prm("final_g", c), "H_ready")

            apply_norm("gmix", H, u, L, rt2, rs2, lambda c: prm("g_mix", c), "gmix_norm")
            n = Tally(S("lam_sums"))
            dve.wait_ge(S("lam_in"), 16)
            for q in range(2):
                n(V_.tensor_tensor_reduce(lam4[:, 2 * q, :], lam4[:, 2 * q, :], lam4[:, 2 * q + 1, :], 1.0, 0.0,
                                          ALU.mult, ALU.add, lam_s[:, q:q + 1]))
            ts(sub_gain, prm("subln"), 1.0 - LAM_INIT, None, ALU.mult).then_inc(S("sub_gain"), 1)
            def qk(e):
                return qb[:, e, :] if e < 8 else kb[:, e - 8, :]

            def normed_head(name, e, head, gain):
                dve.wait_ge(S("head_roots"), HEAD_NORMS[name] + e + 1)
                if e >= 1:
                    dve.wait_ge(S(name + "_normed"), e)
                V_.reciprocal(rs2, rt2).then_inc(S("head_recips"), 1)
                dve.wait_ge(S("head_recips"), HEAD_NORMS[name] + e + 1)
                stt(out=head, in0=head, scalar=gain, in1=rs2, op0=ALU.mult, op1=ALU.mult)\
                    .then_inc(S(name + "_normed"), 1)

            for i in range(13):
                if i < 10:
                    normed_head("qk", i, qk(i), prm("qnorm") if i < 8 else prm("knorm"))
                e = i - 3
                if e >= 0:
                    dve.wait_ge(S("qk_turned"), e + 1)
                    if e >= 2:
                        dve.wait_ge(S("qk_rotated"), e - 1)
                    tt(sined[e % 2], bank(5 + e % 2)[:, 0:L], cst2("rope_sin"), ALU.mult).then_inc(S("qk_sined"), 1)
                    tt(qk(e), qk(e), cst2("rope_cos"), ALU.mult).then_inc(S("qk_cosined"), 1)
                    dve.wait_ge(S("qk_sined"), e + 1)
                    dve.wait_ge(S("qk_cosined"), e + 1)
                    tt(qk(e), qk(e), sined[e % 2], ALU.add).then_inc(S("qk_rotated"), 1)
            dve.wait_ge(S("qk_rotated"), 10)
            for e in range(10):
                dve.wait_ge(S("V_turned"), e + 1)
                V_.tensor_copy(V[:, 0:2, e, :], bank(e % 4)[:, 0:2 * P].rearrange("p (t c) -> p t c", t=2))
                V_.tensor_copy(V[0:16, 2, e, :], bank(e % 4)[0:16, 2 * P:3 * P]).then_inc(S("V_kept"), 1)

            n = Tally(S("lam_steps"))
            dve.wait_ge(S("lam_exp"), 1)
            n(ts(lam_s[:, 4:5], lam_s[:, 2:3], -1.0, -LAM_INIT, ALU.mult, ALU.add))
            n.wait(dve)
            n(tt(lam_s[:, 5:6], lam_s[:, 3:4], lam_s[:, 4:5], ALU.add))
            n.wait(dve)

            biased = Tally(S("biased"))
            maxed = Tally(S("maxed"))
            weighed = Tally(S("weigh_steps"))

            def maxima_and_weights(n):
                un, old = (units[n] if n < len(units) else None), (units[n - 2] if n >= 2 else None)
                if un:
                    nq = QC[un.tile][1]
                    st = stat[n % 3]
                    dve.wait_ge(S("scores"), n + 1)
                    both = ps[0:nq, 2 * (n % 2):2 * (n % 2) + 2, 0:L]
                    if un.diff:
                        slope = 2.0 ** (-8.0 * (un.head + 1) / AH)
                        dist = bc(cst2("dist%d" % un.tile)[0:nq, :].rearrange("p (o t) -> p o t", o=1), nq, 2, L)
                        if n >= 2:
                            dve.wait_ge(S("scores_read"), n - 1)
                        biased(stt(out=sc[n % 2][0:nq, :, :], in0=dist, scalar=-slope * HEAD ** 0.5, in1=both,
                                   op0=ALU.mult, op1=ALU.add))
                        both = sc[n % 2][0:nq, :, :]
                if old:
                    oq = QC[old.tile][1]
                    so, e = stat[(n - 2) % 3], ee[(n - 2) % 3]
                    dve.wait_ge(S("scores_read"), n - 1)
                    weighed(V_.reciprocal(so[0:oq, 6:8], so[0:oq, 4:6]))
                if un:
                    if un.diff:
                        biased.wait(dve)
                    maxed(V_.tensor_reduce(st[0:nq, 0:2], both, AX, ALU.max))
                if old:
                    weighed.wait(dve)
                    if old.diff:
                        weighed(tt(so[0:oq, 7:8], so[0:oq, 7:8], lam_s[0:oq, 5:6], ALU.mult))
                        weighed(ts(e[0:oq, 0, :], e[0:oq, 0, :], so[0:oq, 6:7], None, ALU.mult))
                    else:
                        for m in range(2):
                            ts(e[0:oq, m, :], e[0:oq, m, :], so[0:oq, 6 + m:7 + m], None, ALU.mult)\
                                .then_inc(S("weights"), 1)
                if un:
                    maxed.wait(dve)
                    ts(st[0:nq, 2:4], st[0:nq, 0:2], -(HEAD ** -0.5 if un.diff else P ** -0.5), None, ALU.mult)\
                        .then_inc(S("maxima"), 1)
                if old and old.diff:
                    weighed.wait(dve)
                    stt(out=e[0:oq, 0, :], in0=e[0:oq, 1, :], scalar=so[0:oq, 7:8], in1=e[0:oq, 0, :], op0=ALU.mult,
                        op1=ALU.add).then_inc(S("weights"), 1)

            for n in range(len(units) + 2):
                maxima_and_weights(n)
            dve.wait_ge(S("sub_gain"), 1)
            for j in range(KD):
                dve.wait_ge(S("branch_b"), j + 1)
                tt(gb[:, j, :], bank(j % 4)[:, 0:L], gb[:, j, :], ALU.mult).then_inc(S("branch_b_taken"), 1)
                normed_head("oa", j, oa[:, j, :], sub_gain)
            n = Tally(S("branch_a_steps"))
            for j in range(KD):
                dve.wait_ge(S("branch_a"), j + 1)
                n(tt(ga[:, j, :], bank(j % 4)[:, 0:L], ga[:, j, :], ALU.mult))
                n.wait(dve)
                dve.wait_ge(S("branch_b_taken"), j + 1)
                n(tt(ga[:, j, :], ga[:, j, :], gb[:, j, :], ALU.add))
            for j in range(KD):
                dve.wait_ge(S("wout2"), j + 1)
                tt(H[:, j, :], bank(j % 4)[:, 0:L], H[:, j, :], ALU.add).then_inc(S("wout2_taken"), 1)
            apply_norm("gffn", H, u, L, rt2, rs2, lambda c: prm("g_ffn", c), "gffn_norm")

            n = Tally(S("router_steps"))
            parts = ((P, 0, 2), (16, 2, 3))
            dve.wait_ge(S("logits"), 1)
            for rows, t0, t1 in parts:
                n(V_.tensor_reduce(rstat[0:rows, t0:t1], bank(0)[0:rows, t0 * NE:t1 * NE]
                                   .rearrange("p (t e) -> p t e", e=NE), AX, ALU.max))
            n.wait(dve)
            for rows, t0, t1 in parts:
                tt(logit[0:rows, t0:t1, :], bank(0)[0:rows, t0 * NE:t1 * NE].rearrange("p (t e) -> p t e", e=NE),
                   bc(rstat[0:rows, t0:t1].rearrange("p (t o) -> p t o", o=1), rows, t1 - t0, NE), ALU.subtract)\
                    .then_inc(S("logits_shifted"), 1)
            dve.wait_ge(S("logits_exp"), 2)
            for rows, t0, t1 in parts:
                n(V_.tensor_reduce(rstat[0:rows, 3 + t0:3 + t1], aff[0:rows, t0:t1, :], AX, ALU.add))
            n.wait(dve)
            for rows, t0, t1 in parts:
                n(V_.reciprocal(rstat[0:rows, 3 + t0:3 + t1], rstat[0:rows, 3 + t0:3 + t1]))
            n.wait(dve)
            for rows, t0, t1 in parts:
                last = tt(aff[0:rows, t0:t1, :], aff[0:rows, t0:t1, :],
                          bc(rstat[0:rows, 3 + t0:3 + t1].rearrange("p (t o) -> p t o", o=1), rows, t1 - t0, NE),
                          ALU.mult)
            last.then_inc(S("aff"), 1)
            e16 = slice(0, NE)
            dve.wait_ge(S("aff_turned"), 1)
            n(V_.tensor_copy(aff_e[e16, :], bank(3)[e16, 0:L]))
            n.wait(dve)
            src = aff_e
            for _ in range((CAP - 1) // 8):
                n(V_.max(top8[e16, :], src[e16, :]))
                n.wait(dve)
                n(V_.match_replace(left[e16, :], top8[e16, :], src[e16, :], -1.0))
                n.wait(dve)
                src = left
            n(V_.max(top8[e16, :], left[e16, :]))
            n.wait(dve)
            last_in = top8[e16, (CAP - 1) % 8:(CAP - 1) % 8 + 1]
            n(ts(above[e16, :], aff_e[e16, :], last_in, None, ALU.is_gt))
            n(ts(equal[e16, :], aff_e[e16, :], last_in, None, ALU.is_equal))
            n.wait(dve)
            n(V_.tensor_reduce(counts[e16, 0:1], above[e16, :], AX, ALU.add))
            n(V_.tensor_tensor_scan(left[e16, :], equal[e16, :], equal[e16, :], 0.0, ALU.add, ALU.max))
            n.wait(dve)
            n(ts(counts[e16, 1:2], counts[e16, 0:1], -1.0, float(CAP), ALU.mult, ALU.add))
            n.wait(dve)
            n(stt(out=equal[e16, :], in0=left[e16, :], scalar=counts[e16, 1:2], in1=equal[e16, :], op0=ALU.is_le,
                  op1=ALU.mult))
            n.wait(dve)
            n(tt(above[e16, :], above[e16, :], equal[e16, :], ALU.add))
            n.wait(dve)
            n(V_.tensor_tensor_scan(left[e16, :], above[e16, :], above[e16, :], 0.0, ALU.add, ALU.max))
            n.wait(dve)
            tt(places[e16, :], left[e16, :], above[e16, :], ALU.mult).then_inc(S("places"), 1)
            dve.wait_ge(S("places_turned"), 1)
            for rows, t0, t1 in parts:
                n(V_.tensor_copy(placeT[0:rows, t0:t1, :], bank(4)[0:rows, t0 * NE:t1 * NE]
                                 .rearrange("p (t e) -> p t e", e=NE)))
            n.wait(dve)
            for t, (t0, nt) in enumerate(QC):
                slot = cst2("slot")[0:nt, :].rearrange("p (o s) -> p o s", o=1)
                n(tt(sel[0:nt, t, :, :], bc(placeT[0:nt, t, :].rearrange("p (e o) -> p e o", o=1), nt, NE, SLOTS),
                     bc(slot, nt, NE, SLOTS), ALU.is_equal))
            n.wait(dve)
            for t, (t0, nt) in enumerate(QC):
                last = tt(selA[0:nt, t, :, :], sel[0:nt, t, :, :],
                          bc(aff[0:nt, t, :].rearrange("p (e o) -> p e o", o=1), nt, NE, SLOTS), ALU.mult)
            last.then_inc(S("selA_ready"), 1)

            def pair(i):
                dve.wait_ge(S("silu"), i + 1)
                dve.wait_ge(S("up_e"), i + 1)
                tt(hid, bank(3), hgate, ALU.mult).then_inc(S("hid"), 1)
                for c in range(KD):
                    dve.wait_ge(S("spread"), i * KD + c + 1)
                    tt(H[:, c, :], bank(6 + c % 2)[:, 0:L], H[:, c, :], ALU.add).then_inc(S("added"), 1)
                dve.wait_ge(S("added"), i * KD + KD)

            with dve.Fori(0, NE // 2) as i:
                pair(i)
            apply_norm("last", H, H, L, rt2, rs2, lambda c: prm("g_final", c), "out_ready")

        @block.gpsimd
        def _(pool):
            G = nc.gpsimd
            tt = G.tensor_tensor
            for d in range(2):
                pool.wait_ge(S("sums"), d + 1)
                tt(cum_before[:, d, :, :], cum[:, d, :, :], cum_before[:, d, :, :], ALU.subtract)\
                    .then_inc(S("sums_before"), 1)
            pool.wait_ge(S("ka_rest"), 1)
            pool.wait_ge(S("kk_unit"), NJ)
            pool.wait_ge(S("proj"), 19)

            def steps(s, outputs):
                at = lambda d: 2 * s + d + 1
                n = Tally(S("keys_staged"), s * 16)
                for d in range(2):
                    t = token_at(s, d, outputs)
                    a = iclr[:, d, :, bass.ds(t, C)]
                    n(tt(T0[d], a, per_channel(prm("k_a", 0, NJ), NJ, C), ALU.mult))
                    n(tt(T1[d], a, kk[:, :, bass.ds(t, C)], ALU.mult))
                    n(G.tensor_copy(V0[d], v[:, :, bass.ds(t, C)]))
                    n.wait(pool)
                    n(tt(T0[d], T0[d], per_channel(ka_rest, NJ, C), ALU.add))
                    n.wait(pool)
                    n(tt(T0[d], T0[d], k[:, :, bass.ds(t, C)], ALU.mult))
                    n.wait(pool)
                    pool.wait_ge(S("decays"), at(d))
                    n(tt(KB[d][:, :, 0, :], T0[d], EI[d], ALU.mult))
                    n(tt(KB[d][:, :, 1, :], T1[d], EI[d], ALU.mult))
                    n.wait(pool)
                    between = cst("headones").rearrange("p (o h c) -> p o h c", o=1, h=2)
                    n(tt(RB[d], bc(KB[d][:, :, 1:2, :], P, NJ, 2, C), bc(between, P, NJ, 2, C), ALU.mult))
                n.wait(pool)
                pool.wait_ge(*turn("values_turned", s, 1))

            with pool.Fori(0, 4) as s:
                steps(s, False)
            with pool.Fori(4, 8) as s:
                steps(s, True)

            for j in range(NG):
                pool.wait_ge(S("ffn_act"), j + 1)
                pool.wait_ge(S("ffn_taps"), 8 * (NG + j + 1))
                tt(g[:, j, :], g[:, j, :], acc[:, (NG + j) % 2, :], ALU.mult).then_inc(S("ffn_mul"), 1)

            pool.wait_ge(*norm_root("final1"))
            pool.dma_start(H[:, :, 0:META], dram["meta"]).then_inc(S("meta_in"), 16)
            pool.dma_start(late, dram["consts2"]).then_inc(S("consts2_in"), 16)
            pool.dma_start(lam4.rearrange("p a b -> p (a b)"), dram["lambdas"].to_broadcast([P, 256]))\
                .then_inc(S("lam_in"), 16)
            pool.wait_ge(S("branch_b"), 1)
            pool.dma_start(router, dram["router"]).then_inc(S("router_in"), 16)


def blocks_of(w, rows, columns):
    k, n = w.shape
    out = []
    for n0 in range(0, n, columns):
        for k0 in range(0, k, rows * P):
            part = w[k0:k0 + rows * P, n0:n0 + columns]
            r, c = part.shape[0] // P, part.shape[1]
            b = np.zeros((P, WBLK), w.dtype)
            b[:, :r * c] = part.reshape(r, P, c).transpose(1, 0, 2).reshape(P, r * c)
            out.append(b)
    return out


def by_channel(v):
    t, c = v.shape
    return np.ascontiguousarray(v.T.reshape(c // P, P, t).transpose(1, 0, 2))


def laid_out(i):
    i = {k: np.asarray(v) for k, v in i.items()}
    f = np.float32
    vec = lambda v: np.asarray(v).reshape(-1, P).T
    params = {
        "ada_b": i["ada_b"][0], "norm1_g": i["norm1_g"][0], "norm2_g": i["norm2_g"][0], "conv": i["rwkv_conv_w"][0],
        "w0": i["decay_w0"][0], "a0": i["iclr_a0"][0], "k_k": i["k_k"][0], "k_a": i["k_a"][0], "r_k": i["r_k"][0],
        "gn_g": i["gn_g"][0], "gn_b": i["gn_b"][0], "fourier_g": i["fourier_g"][0], "ffn_conv": i["ffn_conv_w"][0],
        "ffn_b": i["ffn_conv_b"][0], "final_g": i["final_g"], "g_mix": i["g_mix_2"][0], "subln": i["g_subln_2"][0],
        "qnorm": i["g_qnorm_2"][0], "knorm": i["g_knorm_2"][0], "g_ffn": i["g_ffn_2"][0], "g_final": i["g_final_2"]}
    early = W_IN * 512
    blocks = (blocks_of(i["ada_w"][0][:, :early], 8, 512) + blocks_of(i["w_in"][0], 8, 512) + blocks_of(i["w_out"][0], 8, 512)
              + blocks_of(i["ffn_w_up"][0], 8, 512) + blocks_of(i["ffn_w_down"][0], 8, 512)
              + blocks_of(i["w_in_2"][0], 8, 512) + blocks_of(i["w_branch_b_2"][0], 8, 512)
              + blocks_of(i["w_branch_a_2"][0], 8, 512) + blocks_of(i["w_out_2"][0], 8, 512))
    experts = []
    for e in range(0, NE, 2):
        experts += [blocks_of(i[n][0, e + k], r, c)[0] for n, r, c in
                    (("w_gate_2", 8, 512), ("w_up_2", 8, 512), ("w_down_2", 4, 1024)) for k in range(2)]
    table = constant_tables()

    def apart(w):
        rows = np.zeros((2, 64, 2, w.shape[2]), w.dtype)
        rows[0, :, 0], rows[1, :, 1] = w[0], w[1]
        return rows.reshape(P, -1)

    return {
        "consts": np.ascontiguousarray(np.concatenate([table[n] for n in CONST], axis=1).astype(f)),
        "consts2": np.ascontiguousarray(np.concatenate([table[n] for n in CONST2], axis=1).astype(f)),
        "params": np.ascontiguousarray(np.concatenate([vec(params[n]) for n in PARAM], axis=1)),
        "cond": np.ascontiguousarray(np.stack([vec(i["c"][0]), vec(i["c_ctx"])], axis=2)),
        "tokens": np.concatenate([by_channel(i["ctx"][0]), by_channel(i["x"][0])], axis=2),
        "meta": by_channel(i["meta_tokens_2"]),
        "weights": np.stack(blocks),
        "late_ada": np.ascontiguousarray(i["ada_w"][0][:, early:].reshape(KD, P, -1, PIECE).transpose(2, 1, 0, 3)
                                         .reshape(-1, P, KD * PIECE)),
        "experts": np.stack(experts),
        "decay_w2": apart(i["decay_w2"][0]),
        "iclr_a2": apart(i["iclr_a2"][0]),
        "gate_g2": np.ascontiguousarray(i["gate_g2"][0]),
        "router": np.ascontiguousarray(i["w_router_2"][0].reshape(KD, P, NE).transpose(1, 0, 2)),
        "lambdas": np.concatenate([i[n] for n in ("lambda_q1_2", "lambda_k1_2", "lambda_q2_2", "lambda_k2_2")],
                                  axis=1),
    }


def kernel(**inputs):
    import concourse.bacc as bacc
    from concourse.bass_utils import run_bass_kernel_spmd

    nc = bacc.Bacc("TRN2", target_bir_lowering=False, num_devices=1)
    arrays = laid_out(inputs)
    dram = {k: nc.dram_tensor(k, v.shape, mybir.dt.from_np(v.dtype), kind="ExternalInput").ap()
            for k, v in arrays.items()}
    out = nc.dram_tensor("out", (P, KD, TX), F32, kind="ExternalOutput").ap()
    two_blocks(nc, dram, out)
    r = run_bass_kernel_spmd(nc, [arrays], core_ids=[0])
    got = r.results[0]["out"]
    return np.ascontiguousarray(got.transpose(2, 1, 0).reshape(1, TX, D))
```
